# Optimizing a Trainium2 kernel written in Bass

```python
import jax, jax.numpy as jnp
from jax import lax
import numpy as np
import math

D_MODEL = 1024
BATCH = 1
SEQ = 512
DEPTH = 1

POOL_WIDTH = D_MODEL // 2
POOL_WINDOWS = (2, 4, 8, 16)
N_POOL_GROUPS = len(POOL_WINDOWS)
POOL_GROUP = POOL_WIDTH // N_POOL_GROUPS
N_HEADS = 8
HEAD_DIM = 64
ATTN_WIDTH = N_HEADS * HEAD_DIM
MOBA_BLOCK = 256
MOBA_TOPK = 3
Q_CHUNK = 32
D_FF = 4 * D_MODEL
N_BRANCHES = 2
IN_WIDTH = POOL_WIDTH + 3 * ATTN_WIDTH + N_BRANCHES * D_MODEL
EPS = 1e-6
NEG = -1e30


def rmsnorm(x, g):
    xf = x.astype(jnp.float32)
    y = xf * lax.rsqrt(jnp.mean(xf * xf, axis=-1, keepdims=True) + EPS) * g.astype(jnp.float32)
    return y.astype(x.dtype)

def alibi_slopes(n_heads):
    return jnp.asarray(2.0 ** (-8.0 * np.arange(1, n_heads + 1) / n_heads), dtype=jnp.float32)

def pool_mixer(p, pool_w, pool_scale):
    pf = p.astype(jnp.float32)
    B, S, _ = pf.shape
    cs = jnp.concatenate([jnp.zeros_like(pf[:, :1]), jnp.cumsum(pf, axis=1)], axis=1)
    t = jnp.arange(S)
    outs = []
    for g, w in enumerate(POOL_WINDOWS):
        sl = slice(g * POOL_GROUP, (g + 1) * POOL_GROUP)
        lo = jnp.maximum(t + 1 - w, 0)
        win_sum = cs[:, 1:, sl] - cs[:, lo, sl]
        count = jnp.minimum(t + 1, w).astype(jnp.float32)[None, :, None]
        outs.append(win_sum / count - pf[:, :, sl])
    y = jnp.stack(outs, axis=2)
    y = jnp.einsum('bsgc,gcd->bsgd', y, pool_w.astype(jnp.float32))
    y = y.reshape(B, S, POOL_WIDTH) * pool_scale.astype(jnp.float32)
    return y.astype(p.dtype)

def moba_attention(q, k, v):
    B, S, H, Dh = q.shape
    nb = -(-S // MOBA_BLOCK)
    s_pad = nb * MOBA_BLOCK
    qf = q.transpose(0, 2, 1, 3).astype(jnp.float32) * (HEAD_DIM ** -0.5)
    pad = ((0, 0), (0, 0), (0, s_pad - S), (0, 0))
    kf = jnp.pad(k.transpose(0, 2, 1, 3).astype(jnp.float32), pad)
    vf = jnp.pad(v.transpose(0, 2, 1, 3).astype(jnp.float32), pad)
    kb = kf.reshape(B, H, nb, MOBA_BLOCK, Dh)
    vb = vf.reshape(B, H, nb, MOBA_BLOCK, Dh)
    slope = alibi_slopes(H)[None, :, None, None]
    t = jnp.arange(S)
    qblk = t // MOBA_BLOCK
    k_sel = min(MOBA_TOPK, nb - 1)
    if k_sel > 0:
        kmean = jnp.mean(kb, axis=3)
        gate = jnp.einsum('bhsd,bhnd->bhsn', qf, kmean)
        past = jnp.arange(nb)[None, :] < qblk[:, None]
        gate = jnp.where(past[None, None], gate, NEG)
        _, sel = lax.top_k(gate, k_sel)
    else:
        sel = jnp.zeros((B, H, S, 0), dtype=jnp.int32)
    n_chunks = S // Q_CHUNK
    q_c = qf.reshape(B, H, n_chunks, Q_CHUNK, Dh).transpose(2, 0, 1, 3, 4)
    sel_c = sel.reshape(B, H, n_chunks, Q_CHUNK, k_sel).transpose(2, 0, 1, 3, 4)
    bi = jnp.arange(B)[:, None, None]
    hi = jnp.arange(H)[None, :, None]
    kpos_in = jnp.arange(MOBA_BLOCK)

    def chunk_attn(args):
        c, qc, selc = args
        tq = c * Q_CHUNK + jnp.arange(Q_CHUNK)
        own = (c * Q_CHUNK) // MOBA_BLOCK
        k_own = lax.dynamic_slice_in_dim(kf, own * MOBA_BLOCK, MOBA_BLOCK, axis=2)
        v_own = lax.dynamic_slice_in_dim(vf, own * MOBA_BLOCK, MOBA_BLOCK, axis=2)
        ks = own * MOBA_BLOCK + kpos_in
        dist = (tq[:, None] - ks[None, :]).astype(jnp.float32)
        s_own = jnp.einsum('bhqd,bhkd->bhqk', qc, k_own) - slope * dist[None, None]
        s_own = jnp.where((ks[None, :] <= tq[:, None])[None, None], s_own, NEG)
        scores = [s_own]
        idxs = []
        for j in range(k_sel):
            idx = selc[..., j]
            kg = kb[bi, hi, idx]
            kpos = idx[..., None] * MOBA_BLOCK + kpos_in
            d = (tq[None, None, :, None] - kpos).astype(jnp.float32)
            s = jnp.einsum('bhqd,bhqkd->bhqk', qc, kg) - slope * d
            s = jnp.where((idx < own)[..., None], s, NEG)
            scores.append(s)
            idxs.append(idx)
        p = jax.nn.softmax(jnp.concatenate(scores, axis=-1), axis=-1)
        out = jnp.einsum('bhqk,bhkd->bhqd', p[..., :MOBA_BLOCK], v_own)
        for j, idx in enumerate(idxs):
            vg = vb[bi, hi, idx]
            pj = p[..., (j + 1) * MOBA_BLOCK:(j + 2) * MOBA_BLOCK]
            out = out + jnp.einsum('bhqk,bhqkd->bhqd', pj, vg)
        return out

    out = lax.map(chunk_attn, (jnp.arange(n_chunks), q_c, sel_c))
    out = out.transpose(1, 0, 3, 2, 4).reshape(B, S, H * Dh)
    return out.astype(q.dtype)

def first_inputs(seed: int = 0) -> dict:
    key = jax.random.key(seed)
    ks = jax.random.split(key, 16)
    f32 = jnp.float32

    def nrm(k, shape, fan_in):
        return jax.random.normal(k, shape, f32) * (fan_in ** -0.5)

    def gain(k, shape):
        return 1.0 + 0.02 * jax.random.normal(k, shape, f32)

    L = DEPTH
    return {
        "x": jax.random.normal(ks[0], (BATCH, SEQ, D_MODEL), f32),
        "norm_mix_pre": gain(ks[1], (L, D_MODEL)),
        "w_in": nrm(ks[2], (L, D_MODEL, IN_WIDTH), D_MODEL),
        "b_gate": 0.01 * jax.random.normal(ks[3], (L, N_BRANCHES * D_MODEL), f32),
        "pool_w": nrm(ks[4], (L, N_POOL_GROUPS, POOL_GROUP, POOL_GROUP), POOL_GROUP),
        "pool_scale": gain(ks[5], (L, POOL_WIDTH)),
        "w_branch_pool": nrm(ks[6], (L, POOL_WIDTH, D_MODEL), POOL_WIDTH),
        "w_branch_attn": nrm(ks[7], (L, ATTN_WIDTH, D_MODEL), ATTN_WIDTH),
        "w_out": nrm(ks[8], (L, D_MODEL, D_MODEL), D_MODEL),
        "norm_mix_post": gain(ks[9], (L, D_MODEL)),
        "norm_mlp_pre": gain(ks[10], (L, D_MODEL)),
        "w_up": nrm(ks[11], (L, D_MODEL, D_FF), D_MODEL),
        "w_down": nrm(ks[12], (L, D_FF, D_MODEL), D_FF),
        "norm_mlp_post": gain(ks[13], (L, D_MODEL)),
    }

def first_block(x, norm_mix_pre, w_in, b_gate, pool_w, pool_scale, w_branch_pool, w_branch_attn, w_out,
              norm_mix_post, norm_mlp_pre, w_up, w_down, norm_mlp_post):
    B, S, _ = x.shape
    h = x
    o_q = POOL_WIDTH
    o_k = o_q + ATTN_WIDTH
    o_v = o_k + ATTN_WIDTH
    o_g = o_v + ATTN_WIDTH
    for l in range(DEPTH):
        u = rmsnorm(h, norm_mix_pre[l])
        z = u @ w_in[l]
        p = z[..., :o_q]
        q = z[..., o_q:o_k].reshape(B, S, N_HEADS, HEAD_DIM)
        k = z[..., o_k:o_v].reshape(B, S, N_HEADS, HEAD_DIM)
        v = z[..., o_v:o_g].reshape(B, S, N_HEADS, HEAD_DIM)
        g = z[..., o_g:] + b_gate[l]
        g_pool, g_attn = g[..., :D_MODEL], g[..., D_MODEL:]
        y_pool = pool_mixer(p, pool_w[l], pool_scale[l]) @ w_branch_pool[l]
        y_attn = moba_attention(q, k, v) @ w_branch_attn[l]
        m = jax.nn.sigmoid(g_pool) * y_pool + jax.nn.sigmoid(g_attn) * y_attn
        h = h + rmsnorm(m @ w_out[l], norm_mix_post[l])
        u2 = rmsnorm(h, norm_mlp_pre[l])
        a = jnp.square(jax.nn.relu(u2 @ w_up[l]))
        h = h + rmsnorm(a @ w_down[l], norm_mlp_post[l])
    return h


DEPTH_2 = 2

N_MIXERS = 2
N_DIFF_LAYERS = (DEPTH_2 + 1) // 2
N_SWA_LAYERS = DEPTH_2 // 2

DIFF_HEADS = 8
DIFF_HEAD_DIM = D_MODEL // DIFF_HEADS // 2
DIFF_Q_BLOCK = 128

SWA_Q_HEADS = 16
SWA_KV_HEADS = 4
SWA_GROUP = SWA_Q_HEADS // SWA_KV_HEADS
SWA_HEAD_DIM = D_MODEL // SWA_Q_HEADS
WINDOW = 128
SWA_BLOCK = WINDOW

ROPE_DIM = 64
ROPE_THETA = 10000.0

D_FF_2 = 2816
CONV_WIDTH = 3
PLE_DIM = 256


def rms_norm(x, g):
    xf = x.astype(jnp.float32)
    y = xf * lax.rsqrt(jnp.mean(xf * xf, axis=-1, keepdims=True) + EPS)
    return (y * g.astype(jnp.float32)).astype(x.dtype)

def rope_tables(positions):
    inv_freq = ROPE_THETA ** (-jnp.arange(0, ROPE_DIM, 2, dtype=jnp.float32) / ROPE_DIM)
    ang = positions.astype(jnp.float32)[..., None] * inv_freq
    return jnp.cos(ang), jnp.sin(ang)

def apply_rope(x, cos, sin):
    xf = x.astype(jnp.float32)
    x1, x2 = jnp.split(xf, 2, axis=-1)
    c, s = cos[:, :, None, :], sin[:, :, None, :]
    return jnp.concatenate([x1 * c - x2 * s, x2 * c + x1 * s], axis=-1).astype(x.dtype)

def diff_attention(h, w_qkv, w_o, lam, subln, cos, sin, layer_idx):
    B, S, _ = h.shape
    H, d = DIFF_HEADS, DIFF_HEAD_DIM
    q, k, v = jnp.split(h @ w_qkv, 3, axis=-1)
    q = apply_rope(q.reshape(B, S, 2 * H, d), cos, sin)
    k = apply_rope(k.reshape(B, S, 2 * H, d), cos, sin)
    v = v.reshape(B, S, H, 2 * d)
    lam_init = 0.8 - 0.6 * math.exp(-0.3 * layer_idx)
    lf = lam.astype(jnp.float32)
    lam_full = jnp.exp(jnp.sum(lf[0] * lf[1])) - jnp.exp(jnp.sum(lf[2] * lf[3])) + lam_init
    scale = d ** -0.5
    nb = S // DIFF_Q_BLOCK
    q_blocks = jnp.moveaxis(q.reshape(B, nb, DIFF_Q_BLOCK, 2 * H, d), 1, 0)

    def one_block(qb):
        s = jnp.einsum('bqhd,bkhd->bhqk', qb, k).astype(jnp.float32) * scale
        pr = jax.nn.softmax(s, axis=-1).reshape(B, H, 2, DIFF_Q_BLOCK, S)
        a = (pr[:, :, 0] - lam_full * pr[:, :, 1]).astype(v.dtype)
        return jnp.einsum('bhqk,bkhe->bqhe', a, v)

    o = lax.map(one_block, q_blocks)
    o = jnp.moveaxis(o, 0, 1).reshape(B, S, H, 2 * d)
    o = rms_norm(o, subln) * (1.0 - lam_init)
    return o.reshape(B, S, H * 2 * d) @ w_o

def windowed_gqa(h, w_qkv, w_o, sinks, cos, sin):
    B, S, _ = h.shape
    Hq, Hkv, G, d, L = SWA_Q_HEADS, SWA_KV_HEADS, SWA_GROUP, SWA_HEAD_DIM, SWA_BLOCK
    nb = S // L
    q, k, v = jnp.split(h @ w_qkv, [Hq * d, Hq * d + Hkv * d], axis=-1)
    q = apply_rope(q.reshape(B, S, Hq, d), cos, sin).reshape(B, nb, L, Hkv, G, d)
    k = apply_rope(k.reshape(B, S, Hkv, d), cos, sin)
    v = v.reshape(B, S, Hkv, d)

    def band(t):
        tp = jnp.pad(t, ((0, 0), (L, L), (0, 0), (0, 0))).reshape(B, nb + 2, L, Hkv, d)
        return jnp.concatenate([tp[:, :-2], tp[:, 1:-1], tp[:, 2:]], axis=2)

    kb, vb = band(k), band(v)
    s = jnp.einsum('bnqhgd,bnchd->bnhgqc', q, kb).astype(jnp.float32) * (d ** -0.5)
    blk = jnp.arange(nb)[:, None, None] * L
    qpos = blk + jnp.arange(L)[None, :, None]
    kpos = blk - L + jnp.arange(3 * L)[None, None, :]
    mask = (jnp.abs(kpos - qpos) <= WINDOW) & (kpos >= 0) & (kpos < S)
    s = jnp.where(mask[None, :, None, None], s, -jnp.inf)
    sink = sinks.astype(jnp.float32).reshape(1, 1, Hkv, G, 1, 1)
    m = jnp.maximum(jnp.max(s, axis=-1, keepdims=True), sink)
    e = jnp.exp(s - m)
    pr = e / (jnp.sum(e, axis=-1, keepdims=True) + jnp.exp(sink - m))
    o = jnp.einsum('bnhgqc,bnchd->bnqhgd', pr.astype(v.dtype), vb).reshape(B, S, Hq * d)
    return o @ w_o

def conv_ffn(h, w_up, conv_w, conv_b, w_down):
    S = h.shape[1]
    u = h @ w_up
    pad = CONV_WIDTH // 2
    up = jnp.pad(u, ((0, 0), (pad, pad), (0, 0)))
    u = sum(up[:, t:t + S] * conv_w[t] for t in range(CONV_WIDTH)) + conv_b
    gate, val = jnp.split(u, 2, axis=-1)
    return (jax.nn.silu(gate) * val) @ w_down

def second_inputs(seed: int = 0) -> dict:
    key = jax.random.key(seed)
    ks = jax.random.split(key, 24)
    D = D_MODEL

    def nrm(k, shape, scale):
        return jax.random.normal(k, shape, jnp.float32) * scale

    return {
        "x": nrm(ks[0], (BATCH, SEQ, D), 1.0),
        "p": nrm(ks[1], (DEPTH_2, BATCH, SEQ, PLE_DIM), 1.0),
        "positions": jnp.broadcast_to(jnp.arange(SEQ, dtype=jnp.int32), (BATCH, SEQ)),
        "attn_norm": 1.0 + nrm(ks[2], (DEPTH_2, D), 0.05),
        "ffn_norm": 1.0 + nrm(ks[3], (DEPTH_2, D), 0.05),
        "ple_norm": 1.0 + nrm(ks[4], (DEPTH_2, D), 0.05),
        "final_norm": 1.0 + nrm(ks[5], (D,), 0.05),
        "diff_w_qkv": nrm(ks[6], (N_DIFF_LAYERS, D, 3 * D), D ** -0.5),
        "diff_w_o": nrm(ks[7], (N_DIFF_LAYERS, D, D), D ** -0.5),
        "diff_lambda": nrm(ks[8], (N_DIFF_LAYERS, 4, DIFF_HEAD_DIM), 0.1),
        "diff_subln": 1.0 + nrm(ks[9], (N_DIFF_LAYERS, 2 * DIFF_HEAD_DIM), 0.05),
        "swa_w_qkv": nrm(ks[10], (N_SWA_LAYERS, D, (SWA_Q_HEADS + 2 * SWA_KV_HEADS) * SWA_HEAD_DIM), D ** -0.5),
        "swa_w_o": nrm(ks[11], (N_SWA_LAYERS, SWA_Q_HEADS * SWA_HEAD_DIM, D), D ** -0.5),
        "swa_sinks": nrm(ks[12], (N_SWA_LAYERS, SWA_Q_HEADS), 0.5),
        "ffn_w_up": nrm(ks[13], (DEPTH_2, D, 2 * D_FF_2), D ** -0.5),
        "ffn_conv_w": nrm(ks[14], (DEPTH_2, CONV_WIDTH, 2 * D_FF_2), CONV_WIDTH ** -0.5),
        "ffn_conv_b": nrm(ks[15], (DEPTH_2, 2 * D_FF_2), 0.02),
        "ffn_w_down": nrm(ks[16], (DEPTH_2, D_FF_2, D), D_FF_2 ** -0.5),
        "ple_w_proj": nrm(ks[17], (DEPTH_2, PLE_DIM, D), PLE_DIM ** -0.5),
        "ple_w_gate": nrm(ks[18], (DEPTH_2, D, D), D ** -0.5),
    }

def second_block(x, p, positions, attn_norm, ffn_norm, ple_norm, final_norm,
              diff_w_qkv, diff_w_o, diff_lambda, diff_subln,
              swa_w_qkv, swa_w_o, swa_sinks,
              ffn_w_up, ffn_conv_w, ffn_conv_b, ffn_w_down,
              ple_w_proj, ple_w_gate):
    cos, sin = rope_tables(positions)
    h = x
    for i in range(DEPTH_2):
        j = i // N_MIXERS
        hn = rms_norm(h, attn_norm[i])
        if i % N_MIXERS == 0:
            mix = diff_attention(hn, diff_w_qkv[j], diff_w_o[j], diff_lambda[j], diff_subln[j], cos, sin, i)
        else:
            mix = windowed_gqa(hn, swa_w_qkv[j], swa_w_o[j], swa_sinks[j], cos, sin)
        h = h + mix
        h = h + conv_ffn(rms_norm(h, ffn_norm[i]), ffn_w_up[i], ffn_conv_w[i], ffn_conv_b[i], ffn_w_down[i])
        gate = jax.nn.sigmoid(rms_norm(h, ple_norm[i]) @ ple_w_gate[i])
        h = h + (p[i] @ ple_w_proj[i]) * gate
    return rms_norm(h, final_norm)


def setup_inputs(seed=0):
    out = dict(first_inputs(seed))
    for name, value in second_inputs(seed + 1).items():
        if name != "x":
            out[name + "_2"] = value
    return out


def reference(
    x, norm_mix_pre, w_in, b_gate, pool_w, pool_scale, w_branch_pool, w_branch_attn, w_out,
    norm_mix_post, norm_mlp_pre, w_up, w_down, norm_mlp_post, p_2, positions_2, attn_norm_2,
    ffn_norm_2, ple_norm_2, final_norm_2, diff_w_qkv_2, diff_w_o_2, diff_lambda_2, diff_subln_2,
    swa_w_qkv_2, swa_w_o_2, swa_sinks_2, ffn_w_up_2, ffn_conv_w_2, ffn_conv_b_2, ffn_w_down_2,
    ple_w_proj_2, ple_w_gate_2,
):
    x = first_block(
        x, norm_mix_pre, w_in, b_gate, pool_w, pool_scale, w_branch_pool, w_branch_attn, w_out,
        norm_mix_post, norm_mlp_pre, w_up, w_down, norm_mlp_post,
    )
    return second_block(
        x, p_2, positions_2, attn_norm_2, ffn_norm_2, ple_norm_2, final_norm_2, diff_w_qkv_2,
        diff_w_o_2, diff_lambda_2, diff_subln_2, swa_w_qkv_2, swa_w_o_2, swa_sinks_2,
        ffn_w_up_2, ffn_conv_w_2, ffn_conv_b_2, ffn_w_down_2, ple_w_proj_2, ple_w_gate_2,
    )


_drawn_inputs = setup_inputs


def setup_inputs(seed=0):
    import zlib

    import numpy as np

    out = dict(_drawn_inputs(seed))
    spreads = {}
    factors = {'norm_mix_pre': 3.202,
     'b_gate': 25.634,
     'pool_scale': 11.615,
     'norm_mix_post': 11.205,
     'norm_mlp_pre': 17.527,
     'norm_mlp_post': 13.638,
     'ple_norm_2': 52.101,
     'diff_lambda_2': 5.525,
     'diff_subln_2': 9.155,
     'swa_sinks_2': 29.904,
     'ffn_conv_b_2': 14.106,
     'attn_norm_2': 2.691,
     'ffn_norm_2': 5.331}
    for name, (base, spread) in spreads.items():
        noise = np.random.default_rng([zlib.crc32(name.encode()), seed]).standard_normal(out[name].shape)
        drawn = base * np.exp(spread * noise) if base else spread * noise
        out[name] = __import__('jax').numpy.asarray(drawn.astype(out[name].dtype))
    for name, factor in factors.items():
        out[name] = (out[name] * factor).astype(out[name].dtype)
    return out
```

```python
from contextlib import ExitStack

import numpy as np
import concourse.bass as bass
from concourse import mybir

F = mybir.dt.float32
R = mybir.dt.float32r
I32 = mybir.dt.int32
ACT = mybir.ActivationFunctionType
ALU = mybir.AluOpType
AX = mybir.AxisListType.X

S = 512
NC = 8
EPS = 1e-6
BIG = 3.0e38
NU = 6
LOOK = 4
NP = 3
NT = 5
FF2 = 22

V_COLS = {}


def vec_layout():
    at = 0
    for name, n in (("mix_pre", 8), ("b_gate", 16), ("pool_scale", 4), ("mix_post", 8), ("mlp_pre", 8),
                    ("mlp_post", 8), ("attn", 16), ("ffn", 16), ("ple", 16), ("final", 8), ("subln", 1),
                    ("cw", 264), ("cb", 88), ("sinks", 16), ("invf", 1), ("sgn", 1), ("qs", 4),
                    ("icnt", 64)):
        V_COLS[name] = at
        at += n
    return at


NV = vec_layout()


class Eng:

    def __init__(self, key, sem):
        self.key, self.sem, self.n, self.q, self.seen = key, sem, 0, [], {}

    def wait(self, *tokens):
        for t in tokens:
            if t is None:
                continue
            sem, v = t
            if self.seen.get(sem.name, 0) < v:
                self.seen[sem.name] = v
                self.q.append(lambda e, s=sem, v=v: e.wait_ge(s, v))

    def do(self, f, *tokens, sig=True):
        self.wait(*tokens)
        if not sig:
            self.q.append(f)
            return None
        self.n += 1
        self.q.append(lambda e, f=f: f(e).then_inc(self.sem, 1))
        return (self.sem, self.n)

    @property
    def now(self):
        return (self.sem, self.n) if self.n else None

    def run(self, e):
        for f in self.q:
            f(e)


class Pool:

    def __init__(self, views):
        self.views, self.free = dict(enumerate(views)), [(i, ()) for i in range(len(views))]

    def get(self):
        assert self.free, "no buffer is free"
        i, tokens = self.free.pop(0)
        return i, self.views[i], tokens

    def release(self, i, *tokens):
        self.free.append((i, tokens))

    def lend(self, views, *tokens):
        for v in views:
            i = len(self.views)
            self.views[i] = v
            self.free.append((i, tokens))

    def take_back(self, first):
        gone = [x for x in self.free if x[0] >= first]
        self.free = [x for x in self.free if x[0] < first]
        assert len(gone) == len(self.views) - first
        for i, _ in gone:
            del self.views[i]
        return [t for _, ts in gone for t in ts]


def program(nc, A, out):
    order = []
    with ExitStack() as c0:
        build(nc, A, out, None, order, c0, dry=True)
    with ExitStack() as c1:
        build(nc, A, out, order, [], c1, dry=False)


def build(nc, A, out, plan, seen_units, ctx, dry):
    tag = "d" if dry else "m"

    def sb(name, shape, dt):
        return ctx.enter_context(nc.sbuf_tensor(tag + name, shape, dt))

    def sem(name):
        return ctx.enter_context(nc.semaphore(tag + name))

    PE, VE, AC, GP, SP = (Eng(k, sem("s_" + k)) for k in ("pe", "ve", "ac", "gp", "sp"))

    ra = sb("ra", [128, 32, 2, S], R)
    h = sb("h", [128, NC, S], F)
    raw = sb("raw", [128, NP, 2, S], F)
    fa = sb("fa", [128, 8, S], F)
    tmp = sb("tmp", [128, NT, S], F)
    ssq = sb("ssq", [128, S], F)
    rb = sb("rb", [128, S], F)
    mask = sb("mask", [128, S], F)
    rope = sb("rope", [128, 2, S], F)
    ident = sb("ident", [128, 128], F)
    ones = sb("ones", [128, 128], F)
    vec = sb("vec", [128, NV], F)
    sm = sb("sm", [128, 96], F)
    smi = sb("smi", [128, 4], I32)
    gbuf = sb("gbuf", [128, 4, S], F)
    cr = sb("cr", [128, S], F)[:, :]
    sr = sb("sr", [128, S], F)[:, :]
    banks = [ctx.enter_context(nc.psum_tensor(f"{tag}b{i}", [128, S], F)) for i in range(8)]

    def hl(i):
        return ra[:, i, 0, :], ra[:, i, 1, :]

    def vc(name, i):
        return vec[:, V_COLS[name] + i:V_COLS[name] + i + 1]

    U = [hl(i) for i in range(8)]
    WS = [hl(8 + i) for i in range(NU)]
    X0 = 8 + NU

    bank_free = [()] * 8

    dsem = [sem(f"d{i}") for i in range(NP)]
    st = dict(dma=0, split=0, used=0)
    raw_free = [()] * NP
    unit_tok = {}
    unit_free = {}
    total = len(plan) * 2 if plan else 0

    def emit_dma(n):
        slot = n % NP
        SP.wait(*raw_free[slot])
        name, i = plan[n]
        SP.q.append(lambda e: e.dma_start(raw[:, slot, :, :].rearrange("p a b -> p (a b)"),
                                          A[name][i]).then_inc(dsem[slot], 16))

    def emit_split(u):
        n = u // 2
        slot = n % NP
        landed = (dsem[slot], 16 * (n // NP + 1))
        src = raw[:, slot, u % 2, :]
        wh, wl = WS[u % NU]
        freed = unit_free.get(u - NU)
        th = AC.do(lambda e: e.activation(wh, src, ACT.Copy), landed, freed)
        tl = GP.do(lambda e: e.tensor_tensor(wl, src, wh.bitcast(F), ALU.subtract), landed, freed, th)
        unit_tok[u] = (th, tl)
        if u % 2:
            raw_free[slot] = (tl,)
            if n + NP < len(plan):
                emit_dma(n + NP)

    def next_unit(name, idx):
        u = st["used"]
        st["used"] += 1
        if u % 2 == 0:
            seen_units.append((name, idx // 2))
        if plan is None:
            return u, WS[u % NU], (None, None)
        assert plan[u // 2] == (name, idx // 2), (plan[u // 2], name, idx)
        while st["split"] < min(total, u + 1 + LOOK):
            emit_split(st["split"])
            st["split"] += 1
        return u, WS[u % NU], unit_tok[u]

    def linear(name, G, K, rhs, ntiles, evac, lb, first=0, hooks=None):
        kk = 4 // G
        base = first * K // 4
        step = 0
        for g in range(ntiles // G):
            bs = []
            for _ in range(G):
                b = lb.pop(0)
                lb.append(b)
                bs.append(b)
            for b in bs:
                PE.wait(*bank_free[b])
                bank_free[b] = None
            for ku in range(K // kk):
                u, (wh, wl), tok = next_unit(name, base + g * (K // kk) + ku)
                for q in range(kk):
                    k = ku * kk + q
                    xh, xl, xt = rhs(k)
                    PE.wait(*tok, *xt)
                    for j in range(G):
                        c = (q * G + j) * 128
                        ps = banks[bs[j]][:, :]
                        a, l = wh[:, c:c + 128], wl[:, c:c + 128]
                        PE.do(lambda e, ps=ps, a=a, x=xh, s=(k == 0): e.matmul(ps, a, x, start=s, stop=False), sig=False)
                        PE.do(lambda e, ps=ps, a=a, x=xl: e.matmul(ps, a, x, start=False, stop=False), sig=False)
                        last = PE.do(lambda e, ps=ps, l=l, x=xh, s=(k == K - 1): e.matmul(ps, l, x, start=False, stop=s))
                        if k == K - 1:
                            bank_free[bs[j]] = evac(first + g * G + j, ps, last)
                    if q == kk - 1:
                        unit_free[u] = last
                    if hooks and step in hooks:
                        hooks[step]()
                    step += 1
                    yield

    def run(gen):
        for _ in gen:
            pass

    T = Pool([tmp[:, i, :] for i in range(NT)])
    T.lend([gbuf[:, i, :] for i in range(4)])

    def split(dst, src, tok, eng=None, free=()):
        dh, dl = dst
        a = AC.do(lambda e: e.activation(dh, src, ACT.Copy), *tok, *free)
        b = (eng or VE).do(lambda e: e.tensor_tensor(dl, src, dh.bitcast(F), ALU.subtract), *tok, a, *free)
        return a, b

    STB = 7

    def rstd_cols(src, tok, D, col):
        PE.wait(*bank_free[STB], *tok)
        ps = banks[STB]
        for i in range(4):
            t = PE.do(lambda e, i=i: e.matmul(ps[:, i:i + 1], src[:, 128 * i:128 * i + 128], ones[:, 0:1],
                                              start=True, stop=True))
        bank_free[STB] = None
        x, y, a = sm[:, col + 4:col + 8], sm[:, col:col + 4], sm[:, col + 8:col + 12]
        v = VE.do(lambda e: e.tensor_scalar(x, ps[:, 0:4], 1.0 / D, EPS, ALU.mult, ALU.add), t, VE.now)
        bank_free[STB] = (v,)
        v = VE.do(lambda e: e.tensor_scalar(smi[:, :], x.bitcast(I32), 1, None, ALU.arith_shift_right), v)
        v = VE.do(lambda e: e.tensor_scalar(y.bitcast(I32), smi[:, :], -1.0, float(0x5F3759DF), ALU.mult, ALU.add), v)
        for _ in range(3):
            v = VE.do(lambda e: e.tensor_tensor(a, y, y, ALU.mult), v)
            v = VE.do(lambda e: e.scalar_tensor_tensor(out=a, in0=a, scalar=-0.5, in1=x, op0=ALU.mult, op1=ALU.mult), v)
            v = VE.do(lambda e: e.scalar_tensor_tensor(out=y, in0=a, scalar=1.5, in1=y, op0=ALU.add, op1=ALU.mult), v)
        return v

    def spread(col, tok):
        i, d, free = T.get()
        for q in range(4):
            v = VE.do(lambda e, q=q: e.tensor_scalar(d[:, 128 * q:128 * q + 128], ident[:, :], sm[:, col + q:col + q + 1],
                                                     None, ALU.mult), tok, *free)
        PE.wait(v, *bank_free[STB])
        t = PE.do(lambda e: e.matmul(banks[STB][:, :], ones[:, :], d, start=True, stop=True))
        bank_free[STB] = None
        T.release(i, t)
        return t

    stat = dict(n=0, rb_free=(), ssq_free=())

    def add_square(src, tok):
        if stat["n"] == 0:
            stat["tok"] = AC.do(lambda e: e.activation(ssq[:, :], src, ACT.Square), *tok, *stat["ssq_free"])
        else:
            i, q, free = T.get()
            a = AC.do(lambda e: e.activation(q, src, ACT.Square), *tok, *free)
            stat["tok"] = VE.do(lambda e: e.tensor_tensor(ssq[:, :], ssq[:, :], q, ALU.add), a, stat["tok"])
            T.release(i, stat["tok"])
        stat["n"] += 1

    def cols_now():
        assert stat["n"] == NC
        stat["cols"] = rstd_cols(ssq, (stat["tok"],), 1024.0, 0)
        stat["ssq_free"] = (PE.now,)
        stat["n"] = 0

    def spread_now():
        t = spread(0, stat["cols"])
        stat["rb"] = AC.do(lambda e: e.activation(rb[:, :], banks[STB][:, :], ACT.Copy), t, *stat["rb_free"])
        bank_free[STB] = (stat["rb"],)

    s_in = sem("in")
    nin = [0]

    def load(dst, src, *tok):
        SP.wait(*tok)
        SP.q.append(lambda e: e.dma_start(dst, src).then_inc(s_in, 16))
        nin[0] += 1
        return (s_in, 16 * nin[0])

    load(vec[:, :], A["vec"])
    load(h[:, 0:4, :], A["x"][:, 0:4, :])
    t_x = load(h[:, 4:8, :], A["x"][:, 4:8, :])
    if plan:
        for n in range(min(NP, len(plan))):
            emit_dma(n)
    posi = fa[:, 0, :].bitcast(I32)
    load(posi, A["pos"])
    t_cst = load(mask[:, :], A["alibi"])
    t_x = t_cst

    t1 = GP.do(lambda e: e.memset(ident[:, :], 0.0))
    t_ones = GP.do(lambda e: e.memset(ones[:, :], 1.0))
    t_id = GP.do(lambda e: e.affine_select(out=ident[:, :], in_=ident[:, :], compare_op=ALU.not_equal, fill=1.0,
                                           base=0, pattern=[[-1, 128]], channel_multiplier=1), t1)
    PE.wait(t_id, t_ones)
    VE.wait(t_id)
    AC.wait(t_x)
    VE.wait(t_x)
    GP.wait(t_x)

    h_tok = [()] * NC
    u_tok = [None] * NC

    def make_u(k, gain, free):
        uh, ul = U[k]
        add_square(h[:, k, :], h_tok[k])
        g = vc(*gain)
        a = AC.do(lambda e: e.activation(uh, h[:, k, :], ACT.Copy, scale=g), *h_tok[k], *free)
        b = VE.do(lambda e: e.scalar_tensor_tensor(out=ul, in0=h[:, k, :], scalar=g, in1=uh.bitcast(F),
                                                   op0=ALU.mult, op1=ALU.subtract), a, *h_tok[k], *free)
        u_tok[k] = (a, b)

    def rhs_u(k):
        return (*U[k], u_tok[k])

    for k in range(NC):
        make_u(k, ("mix_pre", k), ())

    def rope_tables():
        two_pi = 2 * np.pi
        def piece(x, bits=12):
            m, ex = np.frexp(x)
            return float(np.ldexp(np.round(m * 2.0 ** bits), int(ex) - bits))
        c1 = piece(two_pi)
        c2 = piece(two_pi - c1)
        c3 = float(np.float32(two_pi - c1 - c2))
        magic = 1.5 * 2.0 ** 23
        pf, ang, n1, nh, nl, r = (fa[:, i, :] for i in range(1, 7))
        v = VE.do(lambda e: e.tensor_copy(pf, posi))
        v = VE.do(lambda e: e.tensor_scalar(ang, pf, vc("invf", 0), None, ALU.mult), v)
        outs = []
        for which, shift, add in ((0, 0.25, np.pi / 2), (1, 0.0, 0.0)):
            v = VE.do(lambda e, shift=shift: e.tensor_scalar(n1, ang, float(1 / two_pi), shift, ALU.mult, ALU.add), v)
            v = VE.do(lambda e: e.tensor_scalar(n1, n1, magic, None, ALU.add), v)
            v = VE.do(lambda e: e.tensor_scalar(n1, n1, magic, None, ALU.subtract), v)
            v = VE.do(lambda e: e.tensor_scalar(nh, n1, 2.0 ** -12, magic, ALU.mult, ALU.add), v)
            v = VE.do(lambda e: e.tensor_scalar(nh, nh, magic, None, ALU.subtract), v)
            v = VE.do(lambda e: e.scalar_tensor_tensor(out=nl, in0=nh, scalar=-4096.0, in1=n1,
                                                       op0=ALU.mult, op1=ALU.add), v)
            src = ang
            for cc in (c1, c2, c3):
                v = VE.do(lambda e, cc=cc, src=src: e.scalar_tensor_tensor(
                    out=r, in0=nh, scalar=-4096.0 * cc, in1=src, op0=ALU.mult, op1=ALU.add), v)
                v = VE.do(lambda e, cc=cc: e.scalar_tensor_tensor(
                    out=r, in0=nl, scalar=-cc, in1=r, op0=ALU.mult, op1=ALU.add), v)
                src = r
            if add:
                v = VE.do(lambda e, add=add: e.tensor_scalar(r, r, add, None, ALU.add), v)
            v = VE.do(lambda e: e.tensor_scalar(r, r, 3.1415925, -3.1415925, ALU.min, ALU.max), v)
            v = AC.do(lambda e, w=which: e.activation(rope[:, w, :], r, ACT.Sin), v)
            outs.append(v)
        v = VE.do(lambda e: e.tensor_scalar(rope[:, 1, :], rope[:, 1, :], vc("sgn", 0), None, ALU.mult), v)
        return v

    t_rope = rope_tables()
    fa_free = (VE.now, AC.now)

    sbk = [2, 3]
    tbk = [4, 5]
    obk = 6

    def rot(l):
        b = l.pop(0)
        l.append(b)
        return b

    SWAP = [(i + 16) % 32 for i in range(32)]

    def attention(kind, nun, spu, lat_t, lat_v, Q, KT, VT, span, O, gen, rate, PTb, o_free):
        acts = {}

        def at(slot, f, pri=1):
            acts.setdefault(slot, []).append((pri, len(acts.get(slot, ())), f))

        P = [[fa[:, 4 * b + i, :] for i in range(4)] for b in range(2)]
        p_free = {}
        pt = [hl(PTb + i) for i in range(4)]
        pt_free = [()]
        p_tok = {}
        small = {}

        def s_tile(t, i, comp=None):
            lo, hi = span(i)
            n = hi - lo
            b = rot(sbk)
            ps = banks[b][:, 0:n]
            qh, ql, row, qt = Q(t)
            kh, kl, krow, kt_ = KT(t)
            if comp is not None:
                row = krow = 64 * comp
            assert row == krow
            PE.wait(*bank_free[b], *qt, *kt_)
            bank_free[b] = None
            qs, ks = slice(128 * i, 128 * i + 128), slice(lo, hi)
            rr = slice(row, row + 64)
            PE.do(lambda e: e.matmul(ps, qh[rr, qs], kh[rr, ks], start=True, stop=False), sig=False)
            PE.do(lambda e: e.matmul(ps, ql[rr, qs], kh[rr, ks], start=False, stop=False), sig=False)
            return b, ps, n, PE.do(lambda e: e.matmul(ps, qh[rr, qs], kl[rr, ks], start=False, stop=True))

        def soft(t, i):
            k = (t % 2) * 4 + i
            if kind == "diff":
                base = 24 + 8 * (k % 4)
                a = P[t % 2][i]
                w = []
                ti, pb, tfree = T.get()
                for comp in range(2):
                    b, ps, n, ts = s_tile(t, i, comp)
                    mx, nm, su = (sm[:, base + 2 * z + comp:base + 2 * z + comp + 1] for z in range(3))
                    v = VE.do(lambda e, mx=mx, ps=ps: e.reduce_max(mx, ps, AX), ts, *p_free.get((k, "s"), ()))
                    v = VE.do(lambda e, mx=mx, nm=nm: e.tensor_scalar(nm, mx, -0.125, None, ALU.mult), v)
                    dst = a if comp == 0 else pb
                    fr = p_free.get(k, ()) if comp == 0 else tfree
                    x = AC.do(lambda e, dst=dst, ps=ps, nm=nm, su=su: e.activation(
                        dst, ps, ACT.Exp, bias=nm, scale=0.125, accum_out=su), v, *fr)
                    bank_free[b] = (x,)
                su2 = sm[:, base + 4:base + 6]
                v = VE.do(lambda e: e.reciprocal(su2, su2), x)
                r1, r2 = su2[:, 0:1], su2[:, 1:2]
                v = VE.do(lambda e: e.tensor_scalar(r2, r2, lam, None, ALU.mult), v)
                v = VE.do(lambda e: e.tensor_scalar(a, a, r1, None, ALU.mult), v)
                v = VE.do(lambda e: e.scalar_tensor_tensor(out=a, in0=pb, scalar=r2, in1=a, op0=ALU.mult,
                                                           op1=ALU.add), v)
                T.release(ti, v)
                p_free[(k, "s")] = (v,)
                p_tok[(t, i)] = v
                return
            base = 24 + 4 * k
            mx, nm, su, es = (sm[:, base + z:base + z + 1] for z in range(4))
            lo, hi = span(i)
            a = P[t % 2][i][:, 0:hi - lo]
            b, ps, n, ts = s_tile(t, i)
            off = moff(i)
            m = mask[:, off:off + n]
            v = VE.do(lambda e: e.tensor_tensor_reduce(a, ps, m, 1.0, -BIG, ALU.add, ALU.max, mx), ts,
                      *p_free.get(k, ()), *p_free.get((k, "s"), ()))
            bank_free[b] = (v,)
            if kind == "moba":
                sl = 2.0 ** -(t + 1)
                v = VE.do(lambda e: e.tensor_scalar(nm, mx, -sl, None, ALU.mult), v)
                x = AC.do(lambda e: e.activation(a, a, ACT.Exp, bias=nm, scale=sl, accum_out=su), v)
                v = VE.do(lambda e: e.reciprocal(su, su), x)
            else:
                s8 = sm[:, 8 + t:9 + t] if False else sink8[:, t:t + 1]
                v = VE.do(lambda e: e.tensor_scalar(nm, mx, s8, -0.125, ALU.max, ALU.mult), v)
                x = AC.do(lambda e: e.activation(a, a, ACT.Exp, bias=nm, scale=0.125, accum_out=su), v)
                x = AC.do(lambda e: e.activation(es, vc("sinks", t), ACT.Exp, bias=nm), v)
                v = VE.do(lambda e: e.tensor_tensor(su, su, es, ALU.add), x)
                v = VE.do(lambda e: e.reciprocal(su, su), v)
            v = VE.do(lambda e: e.tensor_scalar(a, a, su, None, ALU.mult), v)
            p_free[(k, "s")] = (v,)
            p_tok[(t, i)] = v

        def turn(t, i):
            k = (t % 2) * 4 + i
            lo, hi = span(i)
            n = (hi - lo) // 128
            b = rot(tbk)
            PE.wait(*bank_free[b], p_tok[(t, i)])
            a = P[t % 2][i]
            ps = banks[b]
            for q in range(n):
                x = PE.do(lambda e, q=q: e.transpose(ps[:, 128 * q:128 * q + 128], a[:, 128 * q:128 * q + 128],
                                                     ident[:, :]))
            p_free[k] = (x,)
            k0 = lo // 128
            dst = ra[:, PTb + k0:PTb + k0 + n, :, 128 * i:128 * i + 128]
            src = ps[:, 0:128 * n].rearrange("p (a b) -> p a b", b=128)
            y = split((dst[:, :, 0, :], dst[:, :, 1, :]), src, (x,), free=pt_free[0] if i == 0 else ())
            bank_free[b] = y
            small[(t, i)] = y

        def pv(t):
            vh, vl, vt = VT(t)
            PE.wait(*bank_free[obk], *vt, *small[(t, 3)])
            bank_free[obk] = None
            ps = banks[obk]
            first = True
            for kt in range(4):
                qs = [i for i in range(4) if span(i)[0] <= 128 * kt < span(i)[1]]
                a, b = 128 * qs[0], 128 * qs[-1] + 128
                ph, pl = pt[kt]
                vs = slice(128 * kt, 128 * kt + 128)
                for z, (vv, pp) in enumerate(((vh, ph), (vh, pl), (vl, ph))):
                    last = PE.do(lambda e, vv=vv, pp=pp, a=a, b=b, vs=vs, s=first, z=z, kt=kt: e.matmul(
                        ps[:, a:b], vv[:, vs], pp[:, a:b], start=s, stop=(z == 2 and kt == 3),
                        skip_group_check=True))
                    first = False
            pt_free[0] = (last,)
            bank_free[obk] = O(t, ps, last)

        for t in range(nun):
            step = spu // 4
            for i in range(4):
                at(spu * t + step * i, lambda t=t, i=i: soft(t, i), 2)
                at(spu * t + step * i + lat_t, lambda t=t, i=i: turn(t, i), 1)
            at(spu * t + lat_v, lambda t=t: pv(t), 0)
        live = True
        for slot in range(max(acts) + 1):
            for _ in range(rate):
                if live and next(gen, "end") == "end":
                    live = False
            for _, _, f in sorted(acts.get(slot, ()), key=lambda z: z[:2]):
                f()
            while pend and pend[0][0] <= slot + 1000:
                pend.pop(0)[1]()
        run(gen)

    pend = []

    def v_tile(dst, ps, tok, mult):
        i, z, free = T.get()
        v = VE.do(lambda e: e.tensor_tensor(z, ps, rb[:, :], ALU.mult), tok, stat["rb"], *free)

        def turn_v():
            b = rot(tbk)
            PE.wait(*bank_free[b], v)
            for q in range(4):
                x = PE.do(lambda e, q=q: e.transpose(banks[b][:, 128 * q:128 * q + 128], z[:, 128 * q:128 * q + 128],
                                                     ident[:, :]))
            T.release(i, x)
            vtoks[dst] = split(hl(dst), banks[b][:, :], (x,), free=())
            bank_free[b] = vtoks[dst]
        return v, turn_v

    vtoks = {}

    def rope_tile(dst, ps, tok, cr, sr, free, dest):
        i, sh, f1 = T.get()
        j, t1_, f2 = T.get()
        a = VE.do(lambda e: e.stream_shuffle(sh, ps, SWAP), tok, *f1)
        b = VE.do(lambda e: e.tensor_tensor(t1_, ps, cr, ALU.mult), tok, *f2, t_cr[0])
        g = GP.do(lambda e: e.tensor_tensor(sh, sh, sr, ALU.mult), a, t_cr[0])
        g = GP.do(lambda e: e.tensor_tensor(t1_, t1_, sh, ALU.add), b, g)
        T.release(i, g)
        y = split(hl(dst), t1_, (g,), eng=GP, free=free)
        T.release(j, *y)
        dest[dst] = y
        return (b, a)

    t_cr = [None]

    QK = X0
    VV = X0 + 4
    OO = X0 + 6
    PY = X0 + 10
    PT1 = X0 + 14
    qk_tok = {}

    def moff(i):
        return moba_off(i)

    def moba_off(i):
        return 384 - 128 * i

    def evac_q1(j):
        def f(_, ps, tok):
            i, z, free = T.get()
            v = VE.do(lambda e: e.scalar_tensor_tensor(out=z, in0=ps, scalar=vc("qs", j), in1=rb[:, :],
                                                       op0=ALU.mult, op1=ALU.mult), tok, stat["rb"], *free)
            y = split(hl(QK + (j % 2) * 2), z, (v,), eng=GP, free=(PE.now,))
            T.release(i, *y)
            qk_tok[("q", j)] = y
            return (v,)
        return f

    def evac_k1(j):
        def f(_, ps, tok):
            i, z, free = T.get()
            v = VE.do(lambda e: e.tensor_tensor(z, ps, rb[:, :], ALU.mult), tok, stat["rb"], *free)
            y = split(hl(QK + (j % 2) * 2 + 1), z, (v,), eng=GP, free=(PE.now,))
            T.release(i, *y)
            qk_tok[("k", j)] = y
            return (v,)
        return f

    def evac_v(dst, key):
        def f(_, ps, tok):
            v, turn_v = v_tile(dst, ps, tok, None)
            turns.append((turn_v, key))
            return (v,)
        return f

    turns = []

    def flush_turns():
        while turns:
            f, key = turns.pop(0)
            f()
            qk_tok[key] = vtoks[key[2]]

    def proj1(j, hooks=None):
        lb = LB2
        n = 0
        for name, ev in (("w_q", evac_q1(j)), ("w_k", evac_k1(j)), ("w_v", evac_v(VV + j % 2, ("v", j, VV + j % 2)))):
            for _ in linear(name, 1, 8, rhs_u, 1, ev, lb, first=j, hooks=hooks if n == 0 else None):
                n += 1
                if n % 8 == 3:
                    flush_turns()
                yield

    LB2 = [0, 1]
    run(proj1(0, {3: cols_now, 7: spread_now} and {6: lambda: (cols_now(), spread_now())}))
    flush_turns()

    def gen1():
        for j in range(1, 4):
            yield from proj1(j)
        yield from linear("w_p", 1, 8, rhs_u, 4, evac_p, LB2, hooks={2: flush_turns})
        flush_turns()

    p_in = {}

    def evac_p(g, ps, tok):
        i0, x, f0 = T.get()
        v = VE.do(lambda e: e.tensor_tensor(x, ps, rb[:, :], ALU.mult), tok, stat["rb"], *f0)
        freed = v
        i1, a, f1 = T.get()
        i2, b, f2 = T.get()
        src, dst, oth = x, a, b
        VE.wait(*f1, *f2)
        for s in range(g + 1):
            d = 1 << s
            v0 = VE.do(lambda e, d=d, src=src, dst=dst: e.tensor_tensor(dst[:, d:S], src[:, d:S], src[:, 0:S - d],
                                                                        ALU.add), v)
            v1 = VE.do(lambda e, d=d, src=src, dst=dst: e.tensor_copy(dst[:, 0:d], src[:, 0:d]), v)
            v = v1
            src, dst, oth = dst, oth, dst
        w = 2 << g
        c = V_COLS["icnt"] + 16 * g
        v = VE.do(lambda e: e.tensor_tensor(dst[:, 0:16], src[:, 0:16], vec[:, c:c + 16], ALU.mult), v)
        v = VE.do(lambda e: e.tensor_tensor(dst[:, 0:16], dst[:, 0:16], x[:, 0:16], ALU.subtract), v)
        v = VE.do(lambda e: e.scalar_tensor_tensor(out=dst[:, 16:S], in0=src[:, 16:S], scalar=1.0 / w, in1=x[:, 16:S],
                                                   op0=ALU.mult, op1=ALU.subtract), v)
        y = split(hl(PY + g), dst, (v,))
        T.release(i0, *y)
        T.release(i1, *y)
        T.release(i2, *y)
        p_in[g] = y
        return (freed,)

    o_tok = {}

    def O1(t, ps, tok):
        j, r = t // 2, 64 * (t % 2)
        oh, ol = hl(OO + j)
        y = split((oh[r:r + 64, :], ol[r:r + 64, :]), ps[r:r + 64, :], (tok,))
        o_tok.setdefault(j, ())
        o_tok[j] = o_tok[j] + y
        return y

    def Q1(t):
        j = t // 2
        return (*hl(QK + (j % 2) * 2), 64 * (t % 2), qk_tok[("q", j)])

    def K1(t):
        j = t // 2
        return (*hl(QK + (j % 2) * 2 + 1), 64 * (t % 2), qk_tok[("k", j)])

    def V1(t):
        j = t // 2
        return (*hl(VV + j % 2), qk_tok[("v", j, VV + j % 2)])

    VE.wait(*fa_free)
    AC.wait(*fa_free)
    attention("moba", 8, 4, 2, 6, Q1, K1, V1, lambda i: (0, 128 * (i + 1)), O1, gen1(), 3, PT1, None)

    t_pw = load(raw_pw := fa[:, 0, :], A["pool_w"], PE.now, VE.now, AC.now)
    pwh, pwl = hl(QK)
    pw_tok = split((pwh, pwl), raw_pw, (t_pw,), free=(PE.now,))
    for g in range(4):
        b = rot(LB2)
        gh, gl = hl(PY + g)
        PE.wait(*bank_free[b], *pw_tok, *p_in[g])
        ps = banks[b]
        cs = slice(128 * g, 128 * g + 128)
        PE.do(lambda e, ps=ps, cs=cs, gh=gh: e.matmul(ps[:, :], pwh[:, cs], gh, start=True, stop=False), sig=False)
        PE.do(lambda e, ps=ps, cs=cs, gl=gl: e.matmul(ps[:, :], pwh[:, cs], gl, start=False, stop=False), sig=False)
        t = PE.do(lambda e, ps=ps, cs=cs, gh=gh: e.matmul(ps[:, :], pwl[:, cs], gh, start=False, stop=True))
        i, z, free = T.get()
        v = VE.do(lambda e, ps=ps, z=z, g=g: e.tensor_scalar(z, ps[:, :], vc("pool_scale", g), None, ALU.mult), t, *free)
        bank_free[b] = (v,)
        p_in[g] = split(hl(PY + g), z, (v,), free=(t,))
        T.release(i, *p_in[g])

    LB7 = [0, 1, 2, 3, 4, 5, 6]
    MM = [QK + i for i in range(6)] + [PT1, PT1 + 1]
    m_tok = {}
    t_mm = PE.now
    sg = {}

    def evac_g(base):
        def f(j, ps, tok):
            i, z, free = T.get()
            v = VE.do(lambda e: e.tensor_tensor(z, ps, rb[:, :], ALU.mult), tok, stat["rb"], *free)
            a = AC.do(lambda e: e.activation(z, z, ACT.Sigmoid, bias=vc("b_gate", base + j)), v)
            sg[(base, j)] = (i, z, a)
            return (v,)
        return f

    def evac_bp(j, ps, tok):
        i, z, a = sg[(0, j)]
        v = VE.do(lambda e: e.tensor_tensor(z, ps, z, ALU.mult), tok, a)
        sg[(0, j)] = (i, z, v)
        return (v,)

    def evac_ba(j, ps, tok):
        i, z, a = sg[(8, j)]
        i0, z0, a0 = sg[(0, j)]
        v = VE.do(lambda e: e.tensor_tensor(z, ps, z, ALU.mult), tok, a)
        w = VE.do(lambda e: e.tensor_tensor(z, z, z0, ALU.add), v, a0)
        T.release(i0, w)
        m_tok[j] = split(hl(MM[j]), z, (w,), free=(t_mm,))
        T.release(i, *m_tok[j])
        return (v,)

    rhs_p = lambda k: (*hl(PY + k), p_in[k])
    rhs_o1 = lambda k: (*hl(OO + k), o_tok[k])
    for jj in range(4):
        run(linear("w_gp", 2, 8, rhs_u, 2, evac_g(0), LB7, first=2 * jj))
        run(linear("w_ga", 2, 8, rhs_u, 2, evac_g(8), LB7, first=2 * jj))
        run(linear("w_bp", 2, 4, rhs_p, 2, evac_bp, LB7, first=2 * jj))
        run(linear("w_ba", 2, 4, rhs_o1, 2, evac_ba, LB7, first=2 * jj))
    stat["rb_free"] = (VE.now,)
    t_u_free = PE.now

    def y_chunk(j):
        return fa[:, j, :]

    y_tok = {}

    def evac_y(j, ps, tok):
        a = AC.do(lambda e: e.activation(y_chunk(j), ps, ACT.Copy), tok)
        y_tok[j] = a
        add_square(y_chunk(j), (a,))
        return (a,)

    def post_norm(gain, nxt, u_free):
        cols_now()
        spread_now()
        for k in range(NC):
            i, z, free = T.get()
            v = VE.do(lambda e, k=k, z=z: e.tensor_tensor(z, y_chunk(k), rb[:, :], ALU.mult), stat["rb"], y_tok[k], *free)
            v = VE.do(lambda e, k=k, z=z: e.scalar_tensor_tensor(out=h[:, k, :], in0=z, scalar=vc(gain, k),
                                                                 in1=h[:, k, :], op0=ALU.mult, op1=ALU.add), v)
            T.release(i, v)
            h_tok[k] = (v,)
            make_u(k, (nxt[0], nxt[1] + k), u_free)
        stat["rb_free"] = (VE.now,)

    rhs_m = lambda k: (*hl(MM[k]), m_tok[k])
    AC.wait(VE.now, PE.now)
    run(linear("w_out4", 4, 8, rhs_m, 4, evac_y, LB7))
    run(linear("w_out1", 1, 8, rhs_m, 4, lambda j, ps, t: evac_y(4 + j, ps, t), LB7))
    post_norm("mix_post", ("mlp_pre", 0), (t_u_free,))

    def a_slot(blk, q):
        return X0 + (blk % 2) * 4 + q

    a_tok = {}
    a_free = {}

    def start_hooks():
        return {1: cols_now, 2: spread_now}

    def evac_up(blk):
        def f(j, ps, tok):
            q = j - 4 * blk
            i, z, free = T.get()
            v = VE.do(lambda e: e.scalar_tensor_tensor(out=z, in0=ps, scalar=0.0, in1=rb[:, :], op0=ALU.max,
                                                       op1=ALU.mult), tok, stat["rb"], *free)
            a = AC.do(lambda e: e.activation(z, z, ACT.Square), v)
            a_tok[(blk, q)] = split(hl(a_slot(blk, q)), z, (a,), free=a_free.get(blk - 2, ()))
            T.release(i, *a_tok[(blk, q)])
            return (v,)
        return f

    def evac_acc(first, last, done):
        def f(j, ps, tok):
            dst = y_chunk(j)
            if first:
                y_tok[j] = AC.do(lambda e: e.activation(dst, ps, ACT.Copy), tok)
                t = y_tok[j]
            else:
                t = y_tok[j] = VE.do(lambda e: e.tensor_tensor(dst, ps, dst, ALU.add), tok, y_tok[j])
            if last:
                done(j)
            return (t,)
        return f

    AC.wait(VE.now)
    t_a0 = PE.now
    a_free[-2] = a_free[-1] = (t_a0,)
    NB = 8
    for b in range(NB + 1):
        if b < NB:
            run(linear("w_up", 4, 8, rhs_u, 4, evac_up(b), LB7, first=4 * b, hooks=start_hooks() if b == 0 else None))
        if b >= 1:
            rh = lambda k, b=b: (*hl(a_slot(b - 1, k)), a_tok[(b - 1, k)])
            run(linear("w_down", 1, 4, rh, 8, lambda j, ps, t, b=b: evac_acc(
                b == 1, b == NB, lambda q: add_square(y_chunk(q), (y_tok[q],)))(j - 8 * (b - 1), ps, t),
                LB7, first=8 * (b - 1)))
            a_free[b - 1] = (PE.now,)
    stat["rb_free"] = (VE.now,)
    post_norm("mlp_post", ("attn", 0), (PE.now,))

    lam = sm[:, 92:93]
    sink8 = sm[:, 76:92]

    def small_consts():
        i, z, free = T.get()
        t = load(z[:, 0:256], A["lam"], *free)
        L = z[:, 0:256].rearrange("p (a b c) -> p a b c", a=2, b=2)
        v = VE.do(lambda e: e.tensor_tensor(z[:, 256:384].rearrange("p (a c) -> p a c", a=2), L[:, :, 0, :], L[:, :, 1, :],
                                            ALU.mult), t)
        v = VE.do(lambda e: e.reduce_sum(z[:, 384:386], z[:, 256:384].rearrange("p (a b) -> p a b", b=64), AX), v)
        a = AC.do(lambda e: e.activation(z[:, 386:388], z[:, 384:386], ACT.Exp), v)
        v = VE.do(lambda e: e.tensor_tensor(lam, z[:, 387:388], z[:, 386:387], ALU.subtract), a)
        v = VE.do(lambda e: e.tensor_scalar(lam, lam, -0.2, None, ALU.add), v)
        T.release(i, v)
        s = V_COLS["sinks"]
        v = VE.do(lambda e: e.tensor_scalar(sink8, vec[:, s:s + 16], 8.0, None, ALU.mult), v)
        return v

    def fold_rope():
        a = VE.do(lambda e: e.tensor_tensor(cr, rope[:, 0, :], rb[:, :], ALU.mult), stat["rb"], t_rope)
        b = VE.do(lambda e: e.tensor_tensor(sr, rope[:, 1, :], rb[:, :], ALU.mult), stat["rb"])
        t_cr[0] = b

    QK, VV, OO, PT2 = X0, X0 + 4, X0 + 6, X0 + 14
    qt, kt_tok = {}, {}
    o_tok2 = {}
    subg = sm[:, 93:94]

    def begin():
        cols_now()
        spread_now()
        fold_rope()

    t_small = small_consts()
    VE.do(lambda e: e.tensor_scalar(subg, vc("subln", 0), 0.8, None, ALU.mult), t_small)

    def proj2(hd, hooks=None):
        base = QK + (hd % 2) * 2
        n = 0
        for name, ev in (
            ("d_q", lambda _, ps, t: rope_tile(base, ps, t, cr, sr, (PE.now,), qt)),
            ("d_k", lambda _, ps, t: rope_tile(base + 1, ps, t, cr, sr, (PE.now,), kt_tok)),
            ("d_v", evac_v(VV + hd % 2, ("v", hd, VV + hd % 2))),
        ):
            for _ in linear(name, 1, 8, rhs_u, 1, ev, LB2, first=hd, hooks=hooks if n == 0 else None):
                n += 1
                if n % 8 == 3:
                    flush_turns()
                yield
        qk_tok[("q2", hd)] = qt[base]
        qk_tok[("k2", hd)] = kt_tok[base + 1]

    run(proj2(0, {6: begin}))
    flush_turns()

    def gen2():
        for j in range(1, 8):
            yield from proj2(j)
        yield
        yield
        yield
        flush_turns()

    def O2(t, ps, tok):
        i, z, f1 = T.get()
        j, q, f2 = T.get()
        z_t = VE.do(lambda e: e.tensor_copy(z, ps[:, :]), tok, *f1)
        a = AC.do(lambda e: e.activation(q, z, ACT.Square), z_t, *f2)

        def later():
            v = rstd_cols(q, (a,), 128.0, 12)
            T.release(j, PE.now)
            s = spread(12, v)
            w = VE.do(lambda e: e.scalar_tensor_tensor(out=z, in0=z, scalar=subg, in1=banks[STB][:, :],
                                                       op0=ALU.mult, op1=ALU.mult), s, z_t)
            bank_free[STB] = (w,)
            o_tok2[t] = split(hl(OO + t), z, (w,))
            T.release(i, *o_tok2[t])
        turns.append((later, ("o", t, "o")))
        vtoks["o"] = None
        return (z_t,)

    AC.wait(VE.now)
    attention("diff", 8, 8, 4, 11,
              lambda t: (*hl(QK + (t % 2) * 2), 0, qk_tok[("q2", t)]),
              lambda t: (*hl(QK + (t % 2) * 2 + 1), 0, qk_tok[("k2", t)]),
              lambda t: (*hl(VV + t % 2), qk_tok[("v", t, VV + t % 2)]),
              lambda i: (0, S), O2, gen2(), 3, PT2, None)
    flush_turns()
    t_uf = PE.now

    def resid(nxt, free):
        def f(j, ps, tok):
            v = VE.do(lambda e: e.tensor_tensor(h[:, j, :], ps, h[:, j, :], ALU.add), tok, *h_tok[j])
            h_tok[j] = (v,)
            make_u(j, (nxt[0], nxt[1] + j), free)
            return (v,)
        return f

    stat["rb_free"] = (VE.now,)
    rhs_o2 = lambda k: (*hl(OO + k), o_tok2[k])

    def out_proj(name, rhs, nxt, free):
        ev = resid(nxt, free)
        run(linear(name + "4", 4, 8, rhs, 4, ev, LB7))
        run(linear(name + "1", 1, 8, rhs, 4, lambda j, ps, t: ev(4 + j, ps, t), LB7))

    out_proj("d_o", rhs_o2, ("ffn", 0), (t_uf,))

    def ffn2(l, nxt_gain):
        gv = {}
        VAL = X0

        def evac_conv(b, val, n):
            def f(j, ps, tok):
                ch = j + (FF2 if val else 0)
                w = [vc("cw", (l * 3 + z) * 2 * FF2 + ch) for z in range(3)]
                cb = vc("cb", l * 2 * FF2 + ch)
                i, z, f1 = T.get()
                q = (j - 4 * b)
                v = VE.do(lambda e: e.tensor_tensor(z, ps, rb[:, :], ALU.mult), tok, stat["rb"], *f1)
                if val:
                    i2, y, f2 = T.get()
                else:
                    i2, y, f2 = None, g_buf[q], g_free.get(q, ())
                a = AC.do(lambda e: e.activation(y, z, ACT.Identity, scale=w[1], bias=cb), v, *f2)
                x = VE.do(lambda e: e.scalar_tensor_tensor(out=y[:, 1:S], in0=z[:, 0:S - 1], scalar=w[0],
                                                           in1=y[:, 1:S], op0=ALU.mult, op1=ALU.add), a)
                x = VE.do(lambda e: e.scalar_tensor_tensor(out=y[:, 0:S - 1], in0=z[:, 1:S], scalar=w[2],
                                                           in1=y[:, 0:S - 1], op0=ALU.mult, op1=ALU.add), x)
                if not val:
                    s = AC.do(lambda e: e.activation(z, y, ACT.Sigmoid), x)
                    gt = GP.do(lambda e: e.tensor_tensor(y, y, z, ALU.mult), s)
                    T.release(i, gt)
                    gv[(b, q)] = gt
                else:
                    T.release(i, x)
                    gb = g_buf[q]
                    m = VE.do(lambda e: e.tensor_tensor(y, y, gb, ALU.mult), x, gv[(b, q)])
                    g_free[q] = (m,)
                    a_tok[(b, q)] = split(hl(a_slot(b, q)), y, (m,), free=a_free.get(b - 2, ()))
                    T.release(i2, *a_tok[(b, q)])
                return (v,)
            return f

        g_buf = [gbuf[:, q, :] for q in range(4)]
        back = tuple(T.take_back(NT))
        g_free = {q: back for q in range(4)}
        a_free.clear()
        a_free[-2] = a_free[-1] = (PE.now,)
        y_tok.clear()
        NBK = 6
        for b in range(NBK + 1):
            if b < NBK:
                G = 4 if b < 5 else 2
                sfx = "" if G == 4 else "t"
                fst = 4 * b if G == 4 else 0
                off = 0 if G == 4 else 20
                run(linear(f"f_g{l}{sfx}", G, 8, rhs_u, G, lambda j, ps, t: evac_conv(b, False, G)(j + off, ps, t), LB7,
                           first=fst, hooks=start_hooks() if b == 0 else None))
                run(linear(f"f_v{l}{sfx}", G, 8, rhs_u, G, lambda j, ps, t: evac_conv(b, True, G)(j + off, ps, t), LB7,
                           first=fst))
            if b >= 1:
                K = 4 if b - 1 < 5 else 2
                rh = lambda k, b=b: (*hl(a_slot(b - 1, k)), a_tok[(b - 1, k)])
                last = b == NBK
                u_free = (PE.now,)

                def done(q):
                    v = VE.do(lambda e, q=q: e.tensor_tensor(h[:, q, :], y_chunk(q), h[:, q, :], ALU.add),
                              y_tok[q], *h_tok[q])
                    h_tok[q] = (v,)
                    make_u(q, ("ple", 8 * l + q), u_free)

                if K == 4:
                    run(linear(f"f_d{l}", 1, 4, rh, 8, lambda j, ps, t, b=b: evac_acc(b == 1, last, done)(
                        j - 8 * (b - 1), ps, t), LB7, first=8 * (b - 1)))
                else:
                    run(linear(f"f_d{l}t", 2, 2, rh, 8, lambda j, ps, t: evac_acc(False, last, done)(j, ps, t), LB7))
                a_free[b - 1] = (PE.now,)
        stat["rb_free"] = (VE.now,)
        t_p = load(gbuf[:, 0:2, :], A["p"][l], VE.now, AC.now, GP.now)
        pts = [split(hl(X0 + 8 + k), gbuf[:, k, :], (t_p,), free=(a_free[-1][0], PE.now)) for k in range(2)]
        pl = {}

        def evac_pp(j, ps, tok):
            pl[j] = AC.do(lambda e: e.activation(y_chunk(j), ps, ACT.Copy), tok, VE.now)
            return (pl[j],)

        rp = lambda k: (*hl(X0 + 8 + k), pts[k])
        uf = []

        def evac_pg(j, ps, tok):
            i, z, f1 = T.get()
            v = VE.do(lambda e: e.tensor_tensor(z, ps, rb[:, :], ALU.mult), tok, stat["rb"], *f1)
            a = AC.do(lambda e: e.activation(z, z, ACT.Sigmoid), v)
            m = VE.do(lambda e: e.tensor_tensor(z, z, y_chunk(j), ALU.mult), a, pl[j])
            m = VE.do(lambda e: e.tensor_tensor(h[:, j, :], h[:, j, :], z, ALU.add), m, *h_tok[j])
            T.release(i, m)
            h_tok[j] = (m,)
            if nxt_gain is None:
                add_square(h[:, j, :], h_tok[j])
            return (v,)

        run(linear(f"p_p{l}", 4, 2, rp, 8, evac_pp, LB7, hooks={3: cols_now}))
        run(linear(f"p_g{l}4", 4, 8, rhs_u, 4, evac_pg, LB7, hooks={1: spread_now}))
        run(linear(f"p_g{l}1", 1, 8, rhs_u, 4, lambda j, ps, t: evac_pg(4 + j, ps, t), LB7))
        if nxt_gain:
            fr = (PE.now,)
            for k in range(NC):
                make_u(k, (nxt_gain[0], nxt_gain[1] + k), fr)
        stat["rb_free"] = (VE.now,)
        T.lend([gbuf[:, q, :] for q in range(4)], pts[0][0], pts[0][1], pts[1][0], pts[1][1])

    AC.wait(VE.now, PE.now)
    ffn2(0, ("attn", 8))

    t_m = load(mask[:, 0:384], A["band"], VE.now)
    VE.wait(t_m)
    QK, KK, VV, OO, PT3 = X0, X0 + 2, X0 + 4, X0 + 6, X0 + 14
    q3, k3 = {}, {}
    fr3 = (PE.now,)

    def proj_kv():
        n = 0
        for j in range(2):
            hk = {6: begin} if j == 0 else None
            yield from linear("s_k", 1, 8, rhs_u, 1, lambda _, ps, t, j=j: rope_tile(KK + j, ps, t, cr, sr, fr3, k3),
                              LB2, first=j, hooks=hk)
        for j in range(2):
            yield from linear("s_v", 1, 8, rhs_u, 1, evac_v(VV + j, ("v", j, VV + j)), LB2, first=j,
                              hooks={3: flush_turns})

    def proj_q(j):
        yield from linear("s_q", 1, 8, rhs_u, 1, lambda _, ps, t: rope_tile(QK + j % 2, ps, t, cr, sr, (PE.now,), q3),
                          LB2, first=j, hooks={3: flush_turns})
        qk_tok[("q3", j)] = q3[QK + j % 2]

    VE.wait(*fr3)
    AC.wait(*fr3)
    run(proj_kv())
    run(proj_q(0))
    flush_turns()

    def gen3():
        for j in range(1, 8):
            yield from proj_q(j)

    o_tok.clear()

    def moff(i):
        return 128 if i == 0 else 0

    def head_of(t):
        j, r = t // 2, t % 2
        return j, r

    def kv_of(t):
        return (t // 2) // 4

    def O3(t, ps, tok):
        j, r = t // 2, 64 * (t % 2)
        oh, ol = hl(OO + j)
        y = split((oh[r:r + 64, :], ol[r:r + 64, :]), ps[r:r + 64, :], (tok,))
        o_tok[j] = o_tok.get(j, ()) + y
        return y

    attention("swa", 16, 4, 3, 7,
              lambda t: (*hl(QK + (t // 2) % 2), 64 * (t % 2), qk_tok[("q3", t // 2)]),
              lambda t: (*hl(KK + kv_of(t)), 64 * (t % 2), k3[KK + kv_of(t)]),
              lambda t: (*hl(VV + kv_of(t)), qk_tok[("v", kv_of(t), VV + kv_of(t))]),
              lambda i: (max(0, 128 * i - 128), min(S, 128 * i + 256)), O3, gen3(), 1, PT3, None)
    stat["rb_free"] = (VE.now,)
    rhs_o3 = lambda k: (*hl(OO + k), o_tok[k])
    out_proj("s_o", rhs_o3, ("ffn", 8), (PE.now,))
    AC.wait(VE.now, PE.now)
    ffn2(1, None)

    cols_now()
    spread_now()
    s_out = sem("out")
    for k in range(NC):
        v = VE.do(lambda e, k=k: e.scalar_tensor_tensor(out=h[:, k, :], in0=h[:, k, :], scalar=vc("final", k),
                                                        in1=rb[:, :], op0=ALU.mult, op1=ALU.mult),
                  stat["rb"], *h_tok[k])
        if k % 2:
            SP.wait(v)
            SP.q.append(lambda e, k=k: e.dma_start(out[:, k - 1:k + 1, :], h[:, k - 1:k + 1, :]).then_inc(s_out, 16))
    SP.wait((s_out, 16 * 4))

    if dry:
        return
    assert st["used"] == total, (st["used"], total)
    block = ctx.enter_context(nc.Block())
    block.sync(SP.run)
    block.gpsimd(GP.run)
    block.scalar(AC.run)
    block.tensor(PE.run)
    block.vector(VE.run)


def lay(w, G):
    K, N = w.shape
    kk = 4 // G
    u = w.reshape(K // 128 // kk, kk, 128, N // (128 * G), 128 * G).transpose(3, 0, 2, 1, 4).reshape(-1, 2, 128, 512)
    return np.ascontiguousarray(u.transpose(0, 2, 1, 3)).reshape(-1, 128, 1024)


def lay_blocks(w, n, G):
    return np.concatenate([lay(w[i:i + n], G) for i in range(0, w.shape[0], n)])


def half_interleave(w):
    K, N = w.shape
    return w.reshape(K, N // 64, 2, 2, 16).transpose(0, 1, 3, 2, 4).reshape(K, N)


SWA_ORDER = [4 * (2 * (j // 4) + r) + j % 4 for j in range(8) for r in range(2)]


def columns(v):
    v = v.reshape(-1, v.shape[-1])
    return np.concatenate([r.reshape(-1, 128).T for r in v], axis=1)


def shape_constants():
    inv = (np.float32(10000.0) ** (-np.arange(0, 64, 2, dtype=np.float32) / np.float32(64))).astype(np.float32)
    p = np.arange(128)
    invf = inv[(p % 64) // 32 * 16 + p % 16][:, None]
    sgn = np.where(p % 32 < 16, -1.0, 1.0).astype(np.float32)[:, None]
    hd = 2 * np.arange(4)[None, :] + (p // 64)[:, None]
    qs = (2.0 ** (hd + 1 - 3)).astype(np.float32)
    t = np.arange(16)
    icnt = np.concatenate([1.0 / np.minimum(t + 1, w) for w in (2, 4, 8, 16)]).astype(np.float32)
    icnt = np.broadcast_to(icnt, (128, 64))
    c = np.arange(512)[None, :] - 384
    d = (p[:, None] - c).astype(np.float32)
    alibi = np.where(d >= 0, -d, np.float32(-BIG)).astype(np.float32)
    c = np.arange(384)[None, :] - 128
    band = np.where(np.abs(c - p[:, None]) <= 128, 0.0, -BIG).astype(np.float32)
    return invf, sgn, qs, icnt, alibi, band


def layout(i):
    i = {k: np.asarray(v) for k, v in i.items()}
    invf, sgn, qs, icnt, alibi, band = shape_constants()
    a = {}
    a["x"] = np.ascontiguousarray(i["x"][0].T.reshape(8, 128, 512).transpose(1, 0, 2))
    a["pos"] = np.ascontiguousarray(np.broadcast_to(i["positions_2"], (128, 512)))
    a["p"] = np.ascontiguousarray(i["p_2"][:, 0].transpose(0, 2, 1).reshape(2, 2, 128, 512).transpose(0, 2, 1, 3))
    a["alibi"], a["band"] = alibi, band
    so = np.array(SWA_ORDER)
    a["vec"] = np.ascontiguousarray(np.concatenate(
        [columns(i[n]) for n in ("norm_mix_pre", "b_gate", "pool_scale", "norm_mix_post", "norm_mlp_pre",
                                 "norm_mlp_post", "attn_norm_2", "ffn_norm_2", "ple_norm_2", "final_norm_2",
                                 "diff_subln_2", "ffn_conv_w_2", "ffn_conv_b_2")]
        + [np.broadcast_to(i["swa_sinks_2"][0][so], (128, 16)), invf, sgn, qs, icnt], axis=1))
    a["lam"] = np.ascontiguousarray(np.broadcast_to(i["diff_lambda_2"][0].reshape(256), (128, 256)))
    w = i["w_in"][0]
    a["w_p"], a["w_q"], a["w_k"], a["w_v"] = (lay(w[:, 512 * n:512 * n + 512], 1) for n in range(4))
    a["w_gp"], a["w_ga"] = lay(w[:, 2048:3072], 2), lay(w[:, 3072:4096], 2)
    a["pool_w"] = np.ascontiguousarray(i["pool_w"][0].transpose(1, 0, 2)).reshape(128, 512)
    a["w_bp"], a["w_ba"] = lay(i["w_branch_pool"][0], 2), lay(i["w_branch_attn"][0], 2)
    a["w_out4"], a["w_out1"] = lay(i["w_out"][0][:, :512], 4), lay(i["w_out"][0][:, 512:], 1)
    a["w_up"] = lay(i["w_up"][0], 4)
    a["w_down"] = lay_blocks(i["w_down"][0], 512, 1)
    w = i["diff_w_qkv_2"][0]
    a["d_q"], a["d_k"], a["d_v"] = (lay(half_interleave(w[:, :1024]), 1), lay(half_interleave(w[:, 1024:2048]), 1),
                                    lay(w[:, 2048:], 1))
    w = i["diff_w_o_2"][0]
    a["d_o4"], a["d_o1"] = lay(w[:, :512], 4), lay(w[:, 512:], 1)
    w = i["swa_w_qkv_2"][0]
    wq = w[:, :1024].reshape(1024, 16, 64)[:, so].reshape(1024, 1024)
    a["s_q"], a["s_k"], a["s_v"] = (lay(half_interleave(wq), 1), lay(half_interleave(w[:, 1024:1280]), 1),
                                    lay(w[:, 1280:], 1))
    w = i["swa_w_o_2"][0].reshape(16, 64, 1024)[so].reshape(1024, 1024)
    a["s_o4"], a["s_o1"] = lay(w[:, :512], 4), lay(w[:, 512:], 1)
    for l in range(2):
        w = i["ffn_w_up_2"][l]
        a[f"f_g{l}"], a[f"f_g{l}t"] = lay(w[:, :2560], 4), lay(w[:, 2560:2816], 2)
        a[f"f_v{l}"], a[f"f_v{l}t"] = lay(w[:, 2816:5376], 4), lay(w[:, 5376:], 2)
        w = i["ffn_w_down_2"][l]
        a[f"f_d{l}"], a[f"f_d{l}t"] = lay_blocks(w[:2560], 512, 1), lay(w[2560:], 2)
        a[f"p_p{l}"] = lay(i["ple_w_proj_2"][l], 4)
        w = i["ple_w_gate_2"][l]
        a[f"p_g{l}4"], a[f"p_g{l}1"] = lay(w[:, :512], 4), lay(w[:, 512:], 1)
    return a


def kernel(**inputs):
    import concourse.bacc as bacc
    from concourse.bass_utils import run_bass_kernel_spmd

    nc = bacc.Bacc("TRN2", target_bir_lowering=False, num_devices=1)
    arrays = {f"in_{k}": v for k, v in layout(inputs).items()}
    aps = {k[3:]: nc.dram_tensor(k, v.shape, mybir.dt.from_np(v.dtype), kind="ExternalInput").ap()
           for k, v in arrays.items()}
    out = nc.dram_tensor("out_dram", (128, 8, 512), F, kind="ExternalOutput").ap()
    program(nc, aps, out)
    r = run_bass_kernel_spmd(nc, [arrays], core_ids=[0])
    got = r.results[0]["out_dram"]
    return np.ascontiguousarray(got.transpose(1, 0, 2).reshape(1024, 512).T)[None]
```

```python
from contextlib import ExitStack

import numpy as np
import concourse.bass as bass
from concourse import mybir

F = mybir.dt.float32
R = mybir.dt.float32r
I32 = mybir.dt.int32
ACT = mybir.ActivationFunctionType
ALU = mybir.AluOpType
AX = mybir.AxisListType.X

S = 512
NC = 8
EPS = 1e-6
BIG = 3.0e38
NU = 6
LOOK = 4
NP = 3
NT = 5
FF2 = 22

V_COLS = {}


def vec_layout():
    at = 0
    for name, n in (("mix_pre", 8), ("b_gate", 16), ("pool_scale", 4), ("mix_post", 8), ("mlp_pre", 8),
                    ("mlp_post", 8), ("attn", 16), ("ffn", 16), ("ple", 16), ("final", 8), ("subln", 1),
                    ("cw", 264), ("cb", 88), ("sinks", 16), ("invf", 1), ("sgn", 1), ("qs", 4),
                    ("icnt", 64)):
        V_COLS[name] = at
        at += n
    return at


NV = vec_layout()


class Eng:

    def __init__(self, key, sem):
        self.key, self.sem, self.n, self.q, self.seen = key, sem, 0, [], {}

    def wait(self, *tokens):
        for t in tokens:
            if t is None:
                continue
            sem, v = t
            if self.seen.get(sem.name, 0) < v:
                self.seen[sem.name] = v
                self.q.append(lambda e, s=sem, v=v: e.wait_ge(s, v))

    def do(self, f, *tokens, sig=True):
        self.wait(*tokens)
        if not sig:
            self.q.append(f)
            return None
        self.n += 1
        self.q.append(lambda e, f=f: f(e).then_inc(self.sem, 1))
        return (self.sem, self.n)

    @property
    def now(self):
        return (self.sem, self.n) if self.n else None

    def run(self, e):
        for f in self.q:
            f(e)


class Pool:

    def __init__(self, views):
        self.views, self.free = dict(enumerate(views)), [(i, ()) for i in range(len(views))]

    def get(self):
        assert self.free, "no buffer is free"
        i, tokens = self.free.pop(0)
        return i, self.views[i], tokens

    def release(self, i, *tokens):
        self.free.append((i, tokens))

    def lend(self, views, *tokens):
        for v in views:
            i = len(self.views)
            self.views[i] = v
            self.free.append((i, tokens))

    def take_back(self, first):
        gone = [x for x in self.free if x[0] >= first]
        self.free = [x for x in self.free if x[0] < first]
        assert len(gone) == len(self.views) - first
        for i, _ in gone:
            del self.views[i]
        return [t for _, ts in gone for t in ts]


def program(nc, A, out):
    order = []
    with ExitStack() as c0:
        build(nc, A, out, None, order, c0, dry=True)
    with ExitStack() as c1:
        build(nc, A, out, order, [], c1, dry=False)


def build(nc, A, out, plan, seen_units, ctx, dry):
    tag = "d" if dry else "m"

    def sb(name, shape, dt):
        return ctx.enter_context(nc.sbuf_tensor(tag + name, shape, dt))

    def sem(name):
        return ctx.enter_context(nc.semaphore(tag + name))

    PE, VE, AC, GP, SP = (Eng(k, sem("s_" + k)) for k in ("pe", "ve", "ac", "gp", "sp"))

    ra = sb("ra", [128, 32, 2, S], R)
    h = sb("h", [128, NC, S], F)
    raw = sb("raw", [128, NP, 2, S], F)
    fa = sb("fa", [128, 8, S], F)
    tmp = sb("tmp", [128, NT, S], F)
    ssq = sb("ssq", [128, S], F)
    rb = sb("rb", [128, S], F)
    mask = sb("mask", [128, S], F)
    rope = sb("rope", [128, 2, S], F)
    ident = sb("ident", [128, 128], F)
    ones = sb("ones", [128, 128], F)
    vec = sb("vec", [128, NV], F)
    sm = sb("sm", [128, 96], F)
    smi = sb("smi", [128, 4], I32)
    gbuf = sb("gbuf", [128, 4, S], F)
    cr = sb("cr", [128, S], F)[:, :]
    sr = sb("sr", [128, S], F)[:, :]
    banks = [ctx.enter_context(nc.psum_tensor(f"{tag}b{i}", [128, S], F)) for i in range(8)]

    def hl(i):
        return ra[:, i, 0, :], ra[:, i, 1, :]

    def vc(name, i):
        return vec[:, V_COLS[name] + i:V_COLS[name] + i + 1]

    U_A = [hl(i) for i in range(8)]
    U_B = [hl(24 + i) for i in range(8)]
    U = list(U_A)
    WS = [hl(8 + i) for i in range(NU)]
    X0 = 8 + NU

    bank_free = [()] * 8

    dsem = [sem(f"d{i}") for i in range(NP)]
    st = dict(dma=0, split=0, used=0)
    raw_free = [()] * NP
    unit_tok = {}
    unit_free = {}
    total = len(plan) * 2 if plan else 0

    def emit_dma(n):
        slot = n % NP
        SP.wait(*raw_free[slot])
        name, i = plan[n]
        SP.q.append(lambda e: e.dma_start(raw[:, slot, :, :].rearrange("p a b -> p (a b)"),
                                          A[name][i]).then_inc(dsem[slot], 16))

    def emit_split(u):
        n = u // 2
        slot = n % NP
        landed = (dsem[slot], 16 * (n // NP + 1))
        src = raw[:, slot, u % 2, :]
        wh, wl = WS[u % NU]
        freed = unit_free.get(u - NU)
        th = AC.do(lambda e: e.activation(wh, src, ACT.Copy), landed, freed)
        tl = GP.do(lambda e: e.tensor_tensor(wl, src, wh.bitcast(F), ALU.subtract), landed, freed, th)
        unit_tok[u] = (th, tl)
        if u % 2:
            raw_free[slot] = (tl,)
            if n + NP < len(plan):
                emit_dma(n + NP)

    def next_unit(name, idx):
        u = st["used"]
        st["used"] += 1
        if u % 2 == 0:
            seen_units.append((name, idx // 2))
        if plan is None:
            return u, WS[u % NU], (None, None)
        assert plan[u // 2] == (name, idx // 2), (plan[u // 2], name, idx)
        while st["split"] < min(total, u + 1 + LOOK):
            emit_split(st["split"])
            st["split"] += 1
        return u, WS[u % NU], unit_tok[u]

    bg = []
    bgn = [0]

    def later(f):
        bg.append(f)

    def tick(n):
        bgn[0] += n
        if bgn[0] >= 9:
            bgn[0] = 0
            if bg:
                bg.pop(0)()

    def flush():
        while bg:
            bg.pop(0)()

    def linear(name, G, K, rhs, ntiles, evac, lb, first=0, hooks=None):
        kk = 4 // G
        base = first * K // 4
        done = []
        step = 0
        for g in range(ntiles // G):
            bs = []
            for _ in range(G):
                b = lb.pop(0)
                lb.append(b)
                bs.append(b)
            for b in bs:
                PE.wait(*bank_free[b])
                bank_free[b] = None
            for ku in range(K // kk):
                u, (wh, wl), tok = next_unit(name, base + g * (K // kk) + ku)
                for q in range(kk):
                    k = ku * kk + q
                    xh, xl, xt = rhs(k)
                    PE.wait(*tok, *xt)
                    for j in range(G):
                        c = (q * G + j) * 128
                        ps = banks[bs[j]][:, :]
                        a, l = wh[:, c:c + 128], wl[:, c:c + 128]
                        PE.do(lambda e, ps=ps, a=a, x=xh, s=(k == 0): e.matmul(ps, a, x, start=s, stop=False), sig=False)
                        PE.do(lambda e, ps=ps, a=a, x=xl: e.matmul(ps, a, x, start=False, stop=False), sig=False)
                        last = PE.do(lambda e, ps=ps, l=l, x=xh, s=(k == K - 1): e.matmul(ps, l, x, start=False, stop=s))
                        if k == K - 1:
                            done.append((j, ps, last))
                    if q == kk - 1:
                        unit_free[u] = last
                    if hooks and step in hooks:
                        hooks[step]()
                    for j, ps, t in done:
                        bank_free[bs[j]] = evac(first + g * G + j, ps, t)
                    done.clear()
                    step += 1
                    tick(3 * G)
                    yield

    def run(gen):
        for _ in gen:
            pass

    def as_ready(gen, ready):
        for k in range(8):
            while not ready(k):
                yield
            next(gen)
            yield
        run(gen)

    T = Pool([tmp[:, i, :] for i in range(NT)])
    T.lend([gbuf[:, i, :] for i in range(4)])

    def split(dst, src, tok, eng=None, free=()):
        dh, dl = dst
        a = AC.do(lambda e: e.activation(dh, src, ACT.Copy), *tok, *free)
        b = (eng or VE).do(lambda e: e.tensor_tensor(dl, src, dh.bitcast(F), ALU.subtract), *tok, a, *free)
        return a, b

    STB = 7

    def rstd_cols(src, tok, D, col):
        PE.wait(*bank_free[STB], *tok)
        ps = banks[STB]
        for i in range(4):
            t = PE.do(lambda e, i=i: e.matmul(ps[:, i:i + 1], src[:, 128 * i:128 * i + 128], ones[:, 0:1],
                                              start=True, stop=True))
        bank_free[STB] = None
        x, y, a = sm[:, col + 4:col + 8], sm[:, col:col + 4], sm[:, col + 8:col + 12]
        v = VE.do(lambda e: e.tensor_scalar(x, ps[:, 0:4], 1.0 / D, EPS, ALU.mult, ALU.add), t, VE.now)
        bank_free[STB] = (v,)
        v = VE.do(lambda e: e.tensor_scalar(smi[:, :], x.bitcast(I32), 1, None, ALU.arith_shift_right), v)
        v = VE.do(lambda e: e.tensor_scalar(y.bitcast(I32), smi[:, :], -1.0, float(0x5F3759DF), ALU.mult, ALU.add), v)
        for _ in range(3):
            v = VE.do(lambda e: e.tensor_tensor(a, y, y, ALU.mult), v)
            v = VE.do(lambda e: e.scalar_tensor_tensor(out=a, in0=a, scalar=-0.5, in1=x, op0=ALU.mult, op1=ALU.mult), v)
            v = VE.do(lambda e: e.scalar_tensor_tensor(out=y, in0=a, scalar=1.5, in1=y, op0=ALU.add, op1=ALU.mult), v)
        return v

    def spread(col, tok):
        i, d, free = T.get()
        for q in range(4):
            v = VE.do(lambda e, q=q: e.tensor_scalar(d[:, 128 * q:128 * q + 128], ident[:, :], sm[:, col + q:col + q + 1],
                                                     None, ALU.mult), tok, *free)
        PE.wait(v, *bank_free[STB])
        t = PE.do(lambda e: e.matmul(banks[STB][:, :], ones[:, :], d, start=True, stop=True))
        bank_free[STB] = None
        T.release(i, t)
        return t

    stat = dict(n=0, rb_free=(), ssq_free=())

    def add_square(src, tok, eng=None):
        if stat["n"] == 0:
            stat["tok"] = AC.do(lambda e: e.activation(ssq[:, :], src, ACT.Square), *tok, *stat["ssq_free"])
        else:
            i, q, free = T.get()
            a = AC.do(lambda e: e.activation(q, src, ACT.Square), *tok, *free)
            stat["tok"] = (eng or VE).do(lambda e: e.tensor_tensor(ssq[:, :], ssq[:, :], q, ALU.add), a, stat["tok"])
            T.release(i, stat["tok"])
        stat["n"] += 1

    def cols_now():
        assert stat["n"] == NC
        stat["cols"] = rstd_cols(ssq, (stat["tok"],), 1024.0, 0)
        stat["ssq_free"] = (PE.now,)
        stat["n"] = 0

    def spread_now():
        t = spread(0, stat["cols"])
        stat["rb"] = AC.do(lambda e: e.activation(rb[:, :], banks[STB][:, :], ACT.Copy), t, *stat["rb_free"])
        bank_free[STB] = (stat["rb"],)

    nin = [0]

    def load(dst, src, *tok):
        SP.wait(*tok)
        s = sem(f"in{nin[0]}")
        nin[0] += 1
        SP.q.append(lambda e: e.dma_start(dst, src).then_inc(s, 16))
        return (s, 16)

    h_tok = [(load(h[:, 0, :], A["x"][:, 0, :]),)]
    t_vec = load(vec[:, :], A["vec"])
    for n, (a, b) in enumerate(((1, 2), (2, 4), (4, 6), (6, 8))):
        if plan and n < NP:
            emit_dma(n)
        h_tok += [(load(h[:, a:b, :], A["x"][:, a:b, :]),)] * (b - a)
    t_cst = load(mask[:, :], A["alibi"])
    t1 = GP.do(lambda e: e.memset(ident[:, :], 0.0))
    t_ones = GP.do(lambda e: e.memset(ones[:, :], 1.0))
    t_id = GP.do(lambda e: e.affine_select(out=ident[:, :], in_=ident[:, :], compare_op=ALU.not_equal, fill=1.0,
                                           base=0, pattern=[[-1, 128]], channel_multiplier=1), t1)
    PE.wait(t_id, t_ones)
    VE.wait(t_id)
    AC.wait(t_vec)
    VE.wait(t_vec, t_cst)

    u_tok = [None] * NC

    def make_u(k, gain, free, eng=None):
        uh, ul = U[k]
        g = vc(*gain)
        a = AC.do(lambda e: e.activation(uh, h[:, k, :], ACT.Copy, scale=g), *h_tok[k], *free)

        def rest():
            b = VE.do(lambda e: e.scalar_tensor_tensor(out=ul, in0=h[:, k, :], scalar=g, in1=uh.bitcast(F),
                                                       op0=ALU.mult, op1=ALU.subtract), a, *h_tok[k], *free)
            u_tok[k] = (a, b)
            add_square(h[:, k, :], h_tok[k], eng)
        return rest

    pending = []
    made = [0]

    def rhs_u(k):
        if k == 0:
            made[0] = 0
        while pending and made[0] <= k + 2:
            pending.pop(0)()
            made[0] += 1
        return (*U[k], u_tok[k])

    rest = None
    for k in range(NC):
        nxt_rest = make_u(k, ("mix_pre", k), ())
        if rest:
            rest()
        rest = nxt_rest
    rest()

    two_pi = 2 * np.pi

    def piece(x, bits=12):
        m, ex = np.frexp(x)
        return float(np.ldexp(np.round(m * 2.0 ** bits), int(ex) - bits))

    c1 = piece(two_pi)
    c2 = piece(two_pi - c1)
    c3 = float(np.float32(two_pi - c1 - c2))
    magic = 1.5 * 2.0 ** 23
    t_rope = []

    def rope_table(which, shift, add):
        def f():
            (i0, ang, f0), (i1, n1, f1), (i2, nh, f2), (i3, r, f3) = (T.get() for _ in range(4))
            t_pos = load(ang.bitcast(I32), A["pos"], *f0)
            VE.wait(*f1, *f2, *f3)
            v = VE.do(lambda e: e.tensor_copy(r, ang.bitcast(I32)), t_pos)
            v = VE.do(lambda e: e.tensor_scalar(ang, r, vc("invf", 0), None, ALU.mult), v)
            v = VE.do(lambda e: e.tensor_scalar(n1, ang, float(1 / two_pi), shift, ALU.mult, ALU.add), v)
            v = VE.do(lambda e: e.tensor_scalar(n1, n1, magic, None, ALU.add), v)
            v = VE.do(lambda e: e.tensor_scalar(n1, n1, magic, None, ALU.subtract), v)
            v = VE.do(lambda e: e.tensor_scalar(nh, n1, 2.0 ** -12, magic, ALU.mult, ALU.add), v)
            v = VE.do(lambda e: e.tensor_scalar(nh, nh, magic, None, ALU.subtract), v)
            v = VE.do(lambda e: e.scalar_tensor_tensor(out=n1, in0=nh, scalar=-4096.0, in1=n1,
                                                       op0=ALU.mult, op1=ALU.add), v)
            src = ang
            for cc in (c1, c2, c3):
                v = VE.do(lambda e, cc=cc, src=src: e.scalar_tensor_tensor(
                    out=r, in0=nh, scalar=-4096.0 * cc, in1=src, op0=ALU.mult, op1=ALU.add), v)
                v = VE.do(lambda e, cc=cc: e.scalar_tensor_tensor(
                    out=r, in0=n1, scalar=-cc, in1=r, op0=ALU.mult, op1=ALU.add), v)
                src = r
            v = VE.do(lambda e: e.tensor_scalar(r, r, add, None, ALU.add), v)
            v = VE.do(lambda e: e.tensor_scalar(r, r, 3.1415925, -3.1415925, ALU.min, ALU.max), v)
            dst = rope[:, which, :]
            v = AC.do(lambda e: e.activation(dst, r, ACT.Sin), v)
            if which:
                v = VE.do(lambda e: e.tensor_scalar(dst, dst, vc("sgn", 0), None, ALU.mult), v)
            for i in (i0, i1, i2, i3):
                T.release(i, v)
            t_rope.append(v)
        return f

    sbk = [2, 3]
    tbk = [4, 5]
    obk = 6

    def rot(l):
        b = l.pop(0)
        l.append(b)
        return b

    SWAP = [(i + 16) % 32 for i in range(32)]

    def attention(kind, nun, spu, lat_t, lat_v, Q, KT, VT, span, O, gen, rate, PTb, drain=None):
        acts = {}

        def at(slot, f, pri=1):
            acts.setdefault(slot, []).append((pri, len(acts.get(slot, ())), f))

        P = [[fa[:, 4 * b + i, :] for i in range(4)] for b in range(2)]
        p_free = {}
        pt = [[ra[:, PTb + 2 * p + z, :, :].rearrange("p a (b c) -> p (a b) c", b=2)
               for z in range(2)] for p in range(2)]
        pt_free = [(), ()]
        p_tok = {}
        small = {}

        def s_tile(t, i, comp=None):
            lo, hi = span(i)
            n = hi - lo
            b = rot(sbk)
            ps = banks[b][:, 0:n]
            qh, ql, row, qt = Q(t)
            kh, kl, krow, kt_ = KT(t)
            if comp is not None:
                row = krow = 64 * comp
            assert row == krow
            PE.wait(*bank_free[b], *qt, *kt_)
            bank_free[b] = None
            qs, ks = slice(128 * i, 128 * i + 128), slice(lo, hi)
            rr = slice(row, row + 64)
            PE.do(lambda e: e.matmul(ps, qh[rr, qs], kh[rr, ks], start=True, stop=False), sig=False)
            PE.do(lambda e: e.matmul(ps, ql[rr, qs], kh[rr, ks], start=False, stop=False), sig=False)
            return b, ps, n, PE.do(lambda e: e.matmul(ps, qh[rr, qs], kl[rr, ks], start=False, stop=True))

        def soft(t, i):
            k = (t % 2) * 4 + i
            free2 = p_free.get((k, "s"), ())
            if kind == "diff":
                base = 24 + 8 * (k % 4)
                a = P[t % 2][i]
                ti, pb, tfree = T.get()
                parts = []
                for comp in range(2):
                    b, ps, n, ts = s_tile(t, i, comp)
                    mx, nm, su = (sm[:, base + 2 * z + comp:base + 2 * z + comp + 1] for z in range(3))
                    v = VE.do(lambda e, mx=mx, ps=ps: e.reduce_max(mx, ps, AX), ts, *free2)
                    v = VE.do(lambda e, mx=mx, nm=nm: e.tensor_scalar(nm, mx, -0.125, None, ALU.mult), v)
                    dst = a if comp == 0 else pb
                    fr = p_free.get(k, ()) if comp == 0 else tfree
                    parts.append((b, dst, ps, nm, su, v, fr))
                su2 = sm[:, base + 4:base + 6]
                d = {}

                def expo():
                    for b, dst, ps, nm, su, v, fr in parts:
                        d["x"] = AC.do(lambda e, dst=dst, ps=ps, nm=nm, su=su: e.activation(
                            dst, ps, ACT.Exp, bias=nm, scale=0.125, accum_out=su), v, *fr)
                        bank_free[b] = (d["x"],)

                def norm():
                    v = VE.do(lambda e: e.reciprocal(su2, su2), d["x"])
                    r1, r2 = su2[:, 0:1], su2[:, 1:2]
                    v = VE.do(lambda e: e.tensor_scalar(r2, r2, lam, None, ALU.mult), v)
                    v = VE.do(lambda e: e.tensor_scalar(a, a, r1, None, ALU.mult), v)
                    v = VE.do(lambda e: e.scalar_tensor_tensor(out=a, in0=pb, scalar=r2, in1=a, op0=ALU.mult,
                                                               op1=ALU.add), v)
                    T.release(ti, v)
                    p_free[(k, "s")] = (v,)
                    p_tok[(t, i)] = v
                return expo, norm
            base = 24 + 4 * k
            mx, nm, su, es = (sm[:, base + z:base + z + 1] for z in range(4))
            lo, hi = span(i)
            a = P[t % 2][i][:, 0:hi - lo]
            b, ps, n, ts = s_tile(t, i)
            off = moff(i)
            m = mask[:, off:off + n]
            v = VE.do(lambda e: e.tensor_tensor_reduce(a, ps, m, 1.0, -BIG, ALU.add, ALU.max, mx), ts,
                      *p_free.get(k, ()), *free2)
            bank_free[b] = (v,)
            if kind == "moba":
                sl, s8 = 2.0 ** -(t + 1), -BIG
            else:
                sl, s8 = 0.125, sink8[:, t:t + 1]
            v = VE.do(lambda e: e.tensor_scalar(nm, mx, s8, -sl, ALU.max, ALU.mult), v)
            d = {}

            def expo():
                d["x"] = AC.do(lambda e: e.activation(a, a, ACT.Exp, bias=nm, scale=sl, accum_out=su), v)
                if kind != "moba":
                    d["x"] = AC.do(lambda e: e.activation(es, vc("sinks", t), ACT.Exp, bias=nm), v)

            def norm():
                v = d["x"]
                if kind != "moba":
                    v = VE.do(lambda e: e.tensor_tensor(su, su, es, ALU.add), v)
                v = VE.do(lambda e: e.reciprocal(su, su), v)
                v = VE.do(lambda e: e.tensor_scalar(a, a, su, None, ALU.mult), v)
                p_free[(k, "s")] = (v,)
                p_tok[(t, i)] = v
            return expo, norm

        def turn(t, i):
            k = (t % 2) * 4 + i
            lo, hi = span(i)
            n = (hi - lo) // 128
            b = rot(tbk)
            PE.wait(*bank_free[b], p_tok[(t, i)])
            a = P[t % 2][i]
            ps = banks[b]
            for q in range(n):
                x = PE.do(lambda e, q=q: e.transpose(ps[:, 128 * q:128 * q + 128], a[:, 128 * q:128 * q + 128],
                                                     ident[:, :]))
            p_free[k] = (x,)
            k0 = lo // 128
            h0 = 128 * (i % 2)
            dst = [pt[i // 2][z][:, k0:k0 + n, h0:h0 + 128] for z in range(2)]
            src = ps[:, 0:128 * n].rearrange("p (a b) -> p a b", b=128)
            free = pt_free[i // 2] if i % 2 == 0 else ()
            hi = AC.do(lambda e: e.activation(dst[0], src, ACT.Copy), x, *free)
            bank_free[b] = None

            def low():
                lo = VE.do(lambda e: e.tensor_tensor(dst[1], src, dst[0].bitcast(F), ALU.subtract), hi)
                bank_free[b] = (lo,)
                small[(t, i)] = (hi, lo)
            sched(1, low)

        def pv(t, pr):
            vh, vl, vt = VT(t)
            PE.wait(*vt, *small[(t, 2 * pr)], *small[(t, 2 * pr + 1)])
            if pr == 0:
                PE.wait(*bank_free[obk])
                bank_free[obk] = None
            ps = banks[obk]
            parts = []
            for kt in range(4):
                qs = [i for i in (2 * pr, 2 * pr + 1) if span(i)[0] <= 128 * kt < span(i)[1]]
                if qs:
                    parts.append((-len(qs), kt, 128 * (qs[0] % 2), 128 * (qs[-1] % 2) + 128))
            parts.sort()
            first = True
            for w, (_, kt, a, b) in enumerate(parts):
                vs = slice(128 * kt, 128 * kt + 128)
                ph, pl = (pt[pr][z][:, kt, a:b] for z in range(2))
                dst = ps[:, 256 * pr + a:256 * pr + b]
                for z, (vv, pp) in enumerate(((vh, ph), (vh, pl), (vl, ph))):
                    last = PE.do(lambda e, vv=vv, pp=pp, dst=dst, vs=vs, s=first, f=(z == 2 and w == len(parts) - 1):
                                 e.matmul(dst, vv[:, vs], pp, start=s, stop=f, skip_group_check=True))
                    first = False
            pt_free[pr] = (last,)
            if pr == 1:
                O(t, ps, last, sched)

        now = [0]

        def sched(d, f):
            at(now[0] + d, f, 0)

        def start(slot, t, i):
            expo, norm = soft(t, i)
            at(slot + 1, expo, 1)
            at(slot + 2, norm, 1)

        for t in range(nun):
            step = spu // 4
            t0 = spu * t + lat_t
            for i in range(4):
                at(spu * t + step * i, lambda t=t, i=i, s=spu * t + step * i: start(s, t, i), 3)
                at(t0 + step * i, lambda t=t, i=i: turn(t, i), 1)
            at(t0 + step + lat_v, lambda t=t: pv(t, 0), 0)
            at(t0 + 3 * step + lat_v, lambda t=t: pv(t, 1), 0)
        live = True
        slot = 0
        while slot <= max(acts):
            now[0] = slot
            if slot == spu * nun and drain:
                assert not live or next(gen, "end") == "end"
                gen, live, rate = drain(), True, lambda slot: 1
            for _ in range(rate(slot)):
                if live and next(gen, "end") == "end":
                    live = False
            if not live:
                tick(9)
            for _, _, f in sorted(acts.get(slot, ()), key=lambda z: z[:2]):
                f()
            slot += 1
        run(gen)
        return PE.now, VE.now, AC.now

    def v_tile(dst, ps, tok, mult):
        i, z, free = T.get()
        v = VE.do(lambda e: e.tensor_tensor(z, ps, rb[:, :], ALU.mult), tok, stat["rb"], *free)

        def turn_v():
            b = rot(tbk)
            PE.wait(*bank_free[b], v)
            for q in range(4):
                x = PE.do(lambda e, q=q: e.transpose(banks[b][:, 128 * q:128 * q + 128], z[:, 128 * q:128 * q + 128],
                                                     ident[:, :]))
            T.release(i, x)
            vtoks[dst] = split(hl(dst), banks[b][:, :], (x,), free=())
            bank_free[b] = vtoks[dst]
        return v, turn_v

    vtoks = {}

    def rope_tile(dst, ps, tok, cr, sr, free, done):
        i, sh, f1 = T.get()
        j, t1_, f2 = T.get()
        a = VE.do(lambda e: e.stream_shuffle(sh, ps, SWAP), tok, *f1)
        b = VE.do(lambda e: e.tensor_tensor(t1_, ps, cr, ALU.mult), tok, *f2, t_cr[0])
        g = GP.do(lambda e: e.tensor_tensor(sh, sh, sr, ALU.mult), a, t_cr[0])
        g = GP.do(lambda e: e.tensor_tensor(t1_, t1_, sh, ALU.add), b, g)
        T.release(i, g)
        def parts():
            y = split(hl(dst), t1_, (g,), eng=GP, free=free)
            T.release(j, *y)
            done(y)
        later(parts)
        return (b, a)

    t_cr = [None]

    QK = X0
    VV = X0 + 4
    OO = X0 + 6
    PY = X0 + 10
    PT1 = X0 + 14
    qk_tok = {}

    def moff(i):
        return moba_off(i)

    def moba_off(i):
        return 384 - 128 * i

    def evac_q1(j):
        def f(_, ps, tok):
            i, z, free = T.get()
            v = VE.do(lambda e: e.scalar_tensor_tensor(out=z, in0=ps, scalar=vc("qs", j), in1=rb[:, :],
                                                       op0=ALU.mult, op1=ALU.mult), tok, stat["rb"], *free)
            y = split(hl(QK + (j % 2) * 2), z, (v,), eng=GP, free=(PE.now,))
            T.release(i, *y)
            qk_tok[("q", j)] = y
            return (v,)
        return f

    def evac_k1(j):
        def f(_, ps, tok):
            i, z, free = T.get()
            v = VE.do(lambda e: e.tensor_tensor(z, ps, rb[:, :], ALU.mult), tok, stat["rb"], *free)
            y = split(hl(QK + (j % 2) * 2 + 1), z, (v,), eng=GP, free=(PE.now,))
            T.release(i, *y)
            qk_tok[("k", j)] = y
            return (v,)
        return f

    def evac_v(dst, key):
        def f(_, ps, tok):
            v, turn_v = v_tile(dst, ps, tok, None)
            turns.append((turn_v, key))
            return (v,)
        return f

    turns = []
    LB2 = [0, 1]

    p_in = {}

    def evac_p(g, ps, tok):
        i0, x, f0 = T.get()
        v = VE.do(lambda e: e.tensor_tensor(x, ps, rb[:, :], ALU.mult), tok, stat["rb"], *f0)
        freed = v
        i1, a, f1 = T.get()
        i2, b, f2 = T.get()
        src, dst, oth = x, a, b
        VE.wait(*f1, *f2)
        for s in range(g + 1):
            d = 1 << s
            v0 = VE.do(lambda e, d=d, src=src, dst=dst: e.tensor_tensor(dst[:, d:S], src[:, d:S], src[:, 0:S - d],
                                                                        ALU.add), v)
            v1 = VE.do(lambda e, d=d, src=src, dst=dst: e.tensor_copy(dst[:, 0:d], src[:, 0:d]), v)
            v = v1
            src, dst, oth = dst, oth, dst
        w = 2 << g
        c = V_COLS["icnt"] + 16 * g
        v = VE.do(lambda e: e.tensor_tensor(dst[:, 0:16], src[:, 0:16], vec[:, c:c + 16], ALU.mult), v)
        v = VE.do(lambda e: e.tensor_tensor(dst[:, 0:16], dst[:, 0:16], x[:, 0:16], ALU.subtract), v)
        v = VE.do(lambda e: e.scalar_tensor_tensor(out=dst[:, 16:S], in0=src[:, 16:S], scalar=1.0 / w, in1=x[:, 16:S],
                                                   op0=ALU.mult, op1=ALU.subtract), v)
        y = split(hl(PY + g), dst, (v,))
        T.release(i0, *y)
        T.release(i1, *y)
        T.release(i2, *y)
        p_in[g] = y
        return (freed,)

    def flush_turns():
        while turns:
            f, key = turns.pop(0)
            f()
            qk_tok[key] = vtoks[key[2]]

    def proj1(j, hooks=None):
        lb = LB2
        n = 0
        for name, ev in (("w_q", evac_q1(j)), ("w_k", evac_k1(j)), ("w_v", evac_v(VV + j % 2, ("v", j, VV + j % 2)))):
            for _ in linear(name, 1, 8, rhs_u, 1, ev, lb, first=j - 1, hooks=hooks if n == 0 else None):
                n += 1
                if n % 8 == 3:
                    flush_turns()
                yield

    LB7 = [0, 1, 2, 3, 4, 5, 6]
    evac_first = (evac_q1(0), evac_k1(0), evac_v(VV, ("v", 0, VV)), lambda _, ps, t: evac_p(0, ps, t))
    run(linear("w_first", 4, 8, rhs_u, 4, lambda j, ps, t: evac_first[j](0, ps, t), [0, 1, 2, 3],
               hooks={6: cols_now, 7: spread_now}))
    flush_turns()

    def gen1():
        for j in range(1, 4):
            yield from proj1(j)
        yield from linear("w_p", 1, 8, rhs_u, 3, lambda j, ps, t: evac_p(j + 1, ps, t), LB2, hooks={2: flush_turns})
        flush_turns()

    o_tok = {}

    def O1(t, ps, tok, sched):
        j, r = t // 2, 64 * (t % 2)
        oh, ol = (z[r:r + 64, :] for z in hl(OO + j))
        src = ps[r:r + 64, :]
        hi = AC.do(lambda e: e.activation(oh, src, ACT.Copy), tok)

        def low():
            lo = VE.do(lambda e: e.tensor_tensor(ol, src, oh.bitcast(F), ALU.subtract), hi)
            bank_free[obk] = (lo,)
            o_tok[j] = o_tok.get(j, ()) + (hi, lo)
        sched(1, low)

    def Q1(t):
        j = t // 2
        return (*hl(QK + (j % 2) * 2), 64 * (t % 2), qk_tok[("q", j)])

    def K1(t):
        j = t // 2
        return (*hl(QK + (j % 2) * 2 + 1), 64 * (t % 2), qk_tok[("k", j)])

    def V1(t):
        j = t // 2
        return (*hl(VV + j % 2), qk_tok[("v", j, VV + j % 2)])

    pw_i, pw_raw, pw_free = T.get()
    t_pw = load(pw_raw, A["pool_w"], *pw_free)
    att_done = attention("moba", 8, 4, 3, 2, Q1, K1, V1, lambda i: (0, 128 * (i + 1)), O1, gen1(), lambda s: 3 if s < 24 else 2, PT1)

    pwh, pwl = hl(PT1 + 2)
    pw_tok = split((pwh, pwl), pw_raw, (t_pw,), free=(att_done[0],))
    T.release(pw_i, *pw_tok)

    def pool_products():
        for g in range(4):
            b = rot(LB7)
            gh, gl = hl(PY + g)
            PE.wait(*bank_free[b], *pw_tok, *p_in[g])
            ps = banks[b]
            cs = slice(128 * g, 128 * g + 128)
            PE.do(lambda e, ps=ps, cs=cs, gh=gh: e.matmul(ps[:, :], pwh[:, cs], gh, start=True, stop=False), sig=False)
            PE.do(lambda e, ps=ps, cs=cs, gl=gl: e.matmul(ps[:, :], pwh[:, cs], gl, start=False, stop=False), sig=False)
            t = PE.do(lambda e, ps=ps, cs=cs, gh=gh: e.matmul(ps[:, :], pwl[:, cs], gh, start=False, stop=True))
            i, z, free = T.get()
            v = VE.do(lambda e, ps=ps, z=z, g=g: e.tensor_scalar(z, ps[:, :], vc("pool_scale", g), None, ALU.mult), t, *free)
            bank_free[b] = (v,)
            p_in[g] = split(hl(PY + g), z, (v,), free=(t,))
            T.release(i, *p_in[g])

    MM = [QK + i for i in range(6)] + [PT1, PT1 + 1]
    m_tok = {}
    t_mm = PE.now
    sg = {}

    def evac_g(base):
        def f(j, ps, tok):
            i, z, free = T.get()
            v = VE.do(lambda e: e.tensor_tensor(z, ps, rb[:, :], ALU.mult), tok, stat["rb"], *free)
            a = AC.do(lambda e: e.activation(z, z, ACT.Sigmoid, bias=vc("b_gate", base + j)), v)
            sg[(base, j)] = (i, z, a)
            return (v,)
        return f

    def evac_bp(j, ps, tok):
        i, z, a = sg[(0, j)]
        v = VE.do(lambda e: e.tensor_tensor(z, ps, z, ALU.mult), tok, a)
        sg[(0, j)] = (i, z, v)
        return (v,)

    def evac_ba(j, ps, tok):
        i, z, a = sg[(8, j)]
        i0, z0, a0 = sg[(0, j)]
        v = VE.do(lambda e: e.tensor_tensor(z, ps, z, ALU.mult), tok, a)
        w = VE.do(lambda e: e.tensor_tensor(z, z, z0, ALU.add), v, a0)
        T.release(i0, w)
        m_tok[j] = split(hl(MM[j]), z, (w,), free=(t_mm,))
        T.release(i, *m_tok[j])
        return (v,)

    rhs_p = lambda k: (*hl(PY + k), p_in[k])
    rhs_o1 = lambda k: (*hl(OO + k), o_tok[k])
    for jj in range(4):
        run(linear("w_gp", 2, 8, rhs_u, 2, evac_g(0), LB7, first=2 * jj))
        run(linear("w_ga", 2, 8, rhs_u, 2, evac_g(8), LB7, first=2 * jj))
        if jj == 0:
            pool_products()
        run(linear("w_bp", 2, 4, rhs_p, 2, evac_bp, LB7, first=2 * jj))
        run(linear("w_ba", 2, 4, rhs_o1, 2, evac_ba, LB7, first=2 * jj))
    stat["rb_free"] = (VE.now,)
    t_u_free = PE.now

    def y_chunk(j):
        return fa[:, j, :]

    y_tok = {}

    def evac_y(j, ps, tok):
        a = AC.do(lambda e: e.activation(y_chunk(j), ps, ACT.Copy), tok)
        y_tok[j] = a
        add_square(y_chunk(j), (a,))
        return (a,)

    def post_norm(gain, nxt, u_free):
        cols_now()
        spread_now()
        def produce(k):
            i, z, free = T.get()
            v = VE.do(lambda e: e.tensor_tensor(z, y_chunk(k), rb[:, :], ALU.mult), stat["rb"], y_tok[k], *free)
            v = VE.do(lambda e: e.scalar_tensor_tensor(out=h[:, k, :], in0=z, scalar=vc(gain, k),
                                                       in1=h[:, k, :], op0=ALU.mult, op1=ALU.add), v)
            T.release(i, v)
            h_tok[k] = (v,)
            if k == NC - 1:
                stat["rb_free"] = (VE.now,)
            return make_u(k, (nxt[0], nxt[1] + k), u_free, GP)

        def chain(k, rest=[None]):
            if k < NC:
                nr = produce(k)
            if rest[0]:
                rest[0]()
            rest[0] = nr if k < NC else None
        for k in range(NC + 1):
            pending.append(lambda k=k: chain(k))

    rhs_m = lambda k: (*hl(MM[k]), m_tok[k])
    AC.wait(*att_done)
    run(linear("w_out4", 4, 8, rhs_m, 4, evac_y, LB7))
    run(linear("w_out1", 1, 8, rhs_m, 4, lambda j, ps, t: evac_y(4 + j, ps, t), LB7))
    post_norm("mix_post", ("mlp_pre", 0), (t_u_free,))

    def a_slot(blk, q):
        return X0 + (blk % 2) * 4 + q

    a_tok = {}
    a_free = {}

    def start_hooks(late=False):
        return {6: cols_now, 7: spread_now} if late else {3: cols_now, 5: spread_now}

    def evac_up(blk):
        def f(j, ps, tok):
            q = j - 4 * blk
            i, z, free = T.get()
            v = VE.do(lambda e: e.scalar_tensor_tensor(out=z, in0=ps, scalar=0.0, in1=rb[:, :], op0=ALU.max,
                                                       op1=ALU.mult), tok, stat["rb"], *free)
            a = AC.do(lambda e: e.activation(z, z, ACT.Square), v)
            a_tok[(blk, q)] = split(hl(a_slot(blk, q)), z, (a,), free=a_free.get(blk - 2, ()))
            T.release(i, *a_tok[(blk, q)])
            return (v,)
        return f

    def evac_acc(first, last, done):
        def f(j, ps, tok):
            dst = y_chunk(j)
            if first:
                y_tok[j] = AC.do(lambda e: e.activation(dst, ps, ACT.Copy), tok, *h_tok[j])
                t = y_tok[j]
            else:
                t = y_tok[j] = VE.do(lambda e: e.tensor_tensor(dst, ps, dst, ALU.add), tok, y_tok[j])
            if last:
                done(j)
            return (t,)
        return f

    t_a0 = PE.now
    a_free[-2] = a_free[-1] = (t_a0,)
    NB = 8
    for b in range(NB + 1):
        if b < NB:
            run(linear("w_up", 4, 8, rhs_u, 4, evac_up(b), LB7, first=4 * b, hooks={0: start_hooks(True), 2: {1: rope_table(0, 0.25, float(np.pi / 2))}, 4: {1: rope_table(1, 0.0, 0.0)}}.get(b)))
        if b >= 1:
            rh = lambda k, b=b: (*hl(a_slot(b - 1, k)), a_tok[(b - 1, k)])
            run(linear("w_down", 1, 4, rh, 8, lambda j, ps, t, b=b: evac_acc(
                b == 1, b == NB, lambda q: add_square(y_chunk(q), (y_tok[q],)))(j - 8 * (b - 1), ps, t),
                LB7, first=8 * (b - 1)))
            a_free[b - 1] = (PE.now,)
    stat["rb_free"] = (VE.now,)
    post_norm("mlp_post", ("attn", 0), (PE.now,))

    lam = sm[:, 92:93]
    sink8 = sm[:, 76:92]

    def small_consts():
        i, z, free = T.get()
        t = load(z[:, 0:256], A["lam"], *free)
        L = z[:, 0:256].rearrange("p (a b c) -> p a b c", a=2, b=2)
        v = VE.do(lambda e: e.tensor_tensor(z[:, 256:384].rearrange("p (a c) -> p a c", a=2), L[:, :, 0, :], L[:, :, 1, :],
                                            ALU.mult), t)
        v = VE.do(lambda e: e.reduce_sum(z[:, 384:386], z[:, 256:384].rearrange("p (a b) -> p a b", b=64), AX), v)
        a = AC.do(lambda e: e.activation(z[:, 386:388], z[:, 384:386], ACT.Exp), v)
        v = VE.do(lambda e: e.tensor_tensor(lam, z[:, 387:388], z[:, 386:387], ALU.subtract), a)
        v = VE.do(lambda e: e.tensor_scalar(lam, lam, -0.2, None, ALU.add), v)
        T.release(i, v)
        s = V_COLS["sinks"]
        v = VE.do(lambda e: e.tensor_scalar(sink8, vec[:, s:s + 16], 8.0, None, ALU.mult), v)
        return v

    def fold_rope():
        a = VE.do(lambda e: e.tensor_tensor(cr, rope[:, 0, :], rb[:, :], ALU.mult), stat["rb"], *t_rope)
        b = VE.do(lambda e: e.tensor_tensor(sr, rope[:, 1, :], rb[:, :], ALU.mult), stat["rb"])
        t_cr[0] = b

    QK, VV, OO, PT2 = X0, X0 + 4, X0 + 6, X0 + 14
    o_tok2 = {}
    subg = sm[:, 93:94]

    def begin():
        spread_now()
        fold_rope()

    t_small = small_consts()
    VE.do(lambda e: e.tensor_scalar(subg, vc("subln", 0), 0.8, None, ALU.mult), t_small)

    def resid(nxt, free):
        def f(j, ps, tok):
            v = VE.do(lambda e: e.tensor_tensor(h[:, j, :], ps, h[:, j, :], ALU.add), tok, *h_tok[j])
            h_tok[j] = (v,)
            later(lambda: later_u(j, nxt, free()))
            return (v,)
        return f

    def later_u(j, nxt, free):
        bg.insert(min(1, len(bg)), make_u(j, (nxt[0], nxt[1] + j), free))

    ev_o = [None]

    def proj2(hd):
        base = QK + (hd % 2) * 2
        n = 0
        for name, ev in ((
            ("d_q", lambda _, ps, t: rope_tile(base, ps, t, cr, sr, (PE.now,),
                                           lambda y: qk_tok.update({("q2", hd): y}))),
            ("d_k", lambda _, ps, t: rope_tile(base + 1, ps, t, cr, sr, (PE.now,),
                                           lambda y: qk_tok.update({("k2", hd): y}))),
            ("d_v", evac_v(VV + hd % 2, ("v", hd, VV + hd % 2))),
        )[1 if hd == 1 else 0:]):
            for _ in linear(name, 1, 8, rhs_u, 1, ev, LB2, first=hd - (2 if name == "d_q" else 1)):
                n += 1
                if n % 8 == 3:
                    flush_turns()
                yield

    rt2 = lambda j, dst, d: lambda _, ps, t: rope_tile(dst, ps, t, cr, sr, (), lambda y: qk_tok.update({d: y}))
    evac_first = (rt2(0, QK, ("q2", 0)), rt2(0, QK + 1, ("k2", 0)), evac_v(VV, ("v", 0, VV)),
                  rt2(1, QK + 2, ("q2", 1)))
    run(linear("d_first", 4, 8, rhs_u, 4, lambda j, ps, t: evac_first[j](0, ps, t), [0, 1, 2, 3], hooks={6: cols_now, 7: begin}))
    flush_turns()
    flush()

    def gen2():
        for j in range(1, 8):
            yield from proj2(j)
        flush_turns()

    def drain2():
        t_uf = PE.now
        ev_o[0] = resid(("ffn", 0), lambda: (t_uf,))
        yield from as_ready(linear("d_o4", 4, 8, lambda k: (*hl(OO + k), o_tok2[k]), 4, ev_o[0], [0, 1, 2, 3]),
                            lambda k: k in o_tok2)

    def O2(t, ps, tok, sched):
        i, z, f1 = T.get()
        z_t = VE.do(lambda e: e.tensor_copy(z, ps[:, :]), tok, *f1)
        bank_free[obk] = (z_t,)
        d = {}

        def square():
            d["j"], d["q"], f2 = T.get()
            d["a"] = AC.do(lambda e: e.activation(d["q"], z, ACT.Square), z_t, *f2)

        def stats():
            d["v"] = rstd_cols(d["q"], (d["a"],), 128.0, 12)
            T.release(d["j"], PE.now)

        def scale():
            s = spread(12, d["v"])
            d["w"] = VE.do(lambda e: e.scalar_tensor_tensor(out=z, in0=z, scalar=subg, in1=banks[STB][:, :],
                                                            op0=ALU.mult, op1=ALU.mult), s, z_t)
            bank_free[STB] = (d["w"],)

        def parts():
            o_tok2[t] = split(hl(OO + t), z, (d["w"],))
            T.release(i, *o_tok2[t])
        for n, f in ((1, square), (2, stats), (4, scale), (5, parts)):
            sched(n, f)

    attention("diff", 8, 8, 4, 3,
              lambda t: (*hl(QK + (t % 2) * 2), 0, qk_tok[("q2", t)]),
              lambda t: (*hl(QK + (t % 2) * 2 + 1), 0, qk_tok[("k2", t)]),
              lambda t: (*hl(VV + t % 2), qk_tok[("v", t, VV + t % 2)]),
              lambda i: (0, S), O2, gen2(), lambda s: 2 if s < 8 else 3, PT2, drain2)
    flush()

    stat["rb_free"] = (VE.now,)
    run(linear("d_o1", 1, 8, lambda k: (*hl(OO + k), o_tok2[k]), 4, lambda j, ps, t: ev_o[0](4 + j, ps, t), LB7))
    flush()

    def ffn2(l, nxt_gain):
        gv = {}
        VAL = X0

        def evac_conv(b, val, n):
            def f(j, ps, tok):
                ch = j + (FF2 if val else 0)
                w = [vc("cw", (l * 3 + z) * 2 * FF2 + ch) for z in range(3)]
                cb = vc("cb", l * 2 * FF2 + ch)
                i, z, f1 = T.get()
                q = (j - 4 * b)
                v = VE.do(lambda e: e.tensor_tensor(z, ps, rb[:, :], ALU.mult), tok, stat["rb"], *f1)
                d = {}

                def one():
                    if val:
                        d["i"], d["y"], f2 = T.get()
                    else:
                        d["y"], f2 = g_buf[q], g_free.get(q, ())
                    y = d["y"]
                    d["a"] = AC.do(lambda e: e.activation(y, z, ACT.Identity, scale=w[1], bias=cb), v, *f2)

                def two():
                    y = d["y"]
                    x = VE.do(lambda e: e.scalar_tensor_tensor(out=y[:, 1:S], in0=z[:, 0:S - 1], scalar=w[0],
                                                               in1=y[:, 1:S], op0=ALU.mult, op1=ALU.add), d["a"])
                    x = VE.do(lambda e: e.scalar_tensor_tensor(out=y[:, 0:S - 1], in0=z[:, 1:S], scalar=w[2],
                                                               in1=y[:, 0:S - 1], op0=ALU.mult, op1=ALU.add), x)
                    if val:
                        T.release(i, x)
                        gb = g_buf[q]
                        x = VE.do(lambda e: e.tensor_tensor(y, y, gb, ALU.mult), x, gv[(b, q)])
                        g_free[q] = (x,)
                    d["x"] = x

                def three():
                    y = d["y"]
                    if val:
                        a_tok[(b, q)] = split(hl(a_slot(b, q)), y, (d["x"],), free=a_free.get(b - 2, ()))
                        T.release(d["i"], *a_tok[(b, q)])
                    else:
                        s = AC.do(lambda e: e.activation(z, y, ACT.Sigmoid), d["x"])
                        gt = GP.do(lambda e: e.tensor_tensor(y, y, z, ALU.mult), s)
                        T.release(i, gt)
                        gv[(b, q)] = gt

                tiles.append((one, two, three))
                if len(tiles) == n:
                    ts = list(tiles)
                    tiles.clear()
                    for s in range(n + 2):
                        later(lambda s=s: [ts[s - z][z]() for z in (2, 1, 0) if 0 <= s - z < n])
                return (v,)
            return f

        tiles = []
        g_buf = [gbuf[:, q, :] for q in range(4)]
        back = tuple(T.take_back(NT))
        T.lend([cr, sr], VE.now, GP.now)
        g_free = {q: back for q in range(4)}
        pts = []
        for k in range(2):
            i, z, free = T.get()
            t_p = load(z, A["p"][l][:, k, :], *free)
            pts.append(split(hl(X0 + 8 + k), z, (t_p,), free=(PE.now,)))
            T.release(i, *pts[k])
        a_free.clear()
        a_free[-2] = a_free[-1] = (PE.now,)
        y_tok.clear()
        NBK = 6
        for b in range(NBK + 1):
            if b < NBK:
                G = 4 if b < 5 else 2
                sfx = "" if G == 4 else "t"
                fst = 4 * b if G == 4 else 0
                off = 0 if G == 4 else 20
                run(linear(f"f_g{l}{sfx}", G, 8, rhs_u, G, lambda j, ps, t: evac_conv(b, False, G)(j + off, ps, t), LB7,
                           first=fst, hooks=start_hooks() if b == 0 else None))
                run(linear(f"f_v{l}{sfx}", G, 8, rhs_u, G, lambda j, ps, t: evac_conv(b, True, G)(j + off, ps, t), LB7,
                           first=fst))
            if b >= 1:
                K = 4 if b - 1 < 5 else 2
                rh = lambda k, b=b: (*hl(a_slot(b - 1, k)), a_tok[(b - 1, k)])
                last = b == NBK
                u_free = (PE.now,)

                def done(q):
                    v = VE.do(lambda e, q=q: e.tensor_tensor(h[:, q, :], y_chunk(q), h[:, q, :], ALU.add),
                              y_tok[q], *h_tok[q])
                    h_tok[q] = (v,)
                    later(lambda: later_u(q, ("ple", 8 * l), u_free))

                if K == 4:
                    run(linear(f"f_d{l}", 1, 4, rh, 8, lambda j, ps, t, b=b: evac_acc(b == 1, last, done)(
                        j - 8 * (b - 1), ps, t), LB7, first=8 * (b - 1)))
                else:
                    run(linear(f"f_d{l}t", 2, 2, rh, 8, lambda j, ps, t: evac_acc(False, last, done)(j, ps, t), LB7))
                a_free[b - 1] = (PE.now,)
        stat["rb_free"] = (VE.now,)
        flush()
        pl = {}

        def evac_pp(j, ps, tok):
            pl[j] = AC.do(lambda e: e.activation(y_chunk(j), ps, ACT.Copy), tok, *h_tok[j])
            return (pl[j],)

        rp = lambda k: (*hl(X0 + 8 + k), pts[k])
        ub_free = (PE.now,)
        def evac_pg(j, ps, tok):
            i, z, f1 = T.get()
            v = VE.do(lambda e: e.tensor_tensor(z, ps, rb[:, :], ALU.mult), tok, stat["rb"], *f1)
            a = AC.do(lambda e: e.activation(z, z, ACT.Sigmoid), v)
            m = VE.do(lambda e: e.tensor_tensor(z, z, y_chunk(j), ALU.mult), a, pl[j])
            m = VE.do(lambda e: e.tensor_tensor(h[:, j, :], h[:, j, :], z, ALU.add), m, *h_tok[j])
            T.release(i, m)
            h_tok[j] = (m,)
            if nxt_gain is None:
                later(lambda: add_square(h[:, j, :], h_tok[j]))
            else:
                later(lambda: later_u(j, nxt_gain, ub_free))
            return (v,)

        run(linear(f"p_p{l}", 4, 2, rp, 8, evac_pp, LB7, hooks={3: cols_now}))
        Uc, uc = list(U), list(u_tok)
        rhs_g = lambda k: (*Uc[k], uc[k])
        if nxt_gain:
            U[:] = U_B
        run(linear(f"p_g{l}4", 4, 8, rhs_g, 4, evac_pg, LB7, hooks={1: spread_now}))
        run(linear(f"p_g{l}1", 1, 8, rhs_g, 4, lambda j, ps, t: evac_pg(4 + j, ps, t), LB7))
        flush()
        stat["rb_free"] = (VE.now,)
        back = tuple(T.take_back(NT))
        T.lend([gbuf[:, q, :] for q in range(4)], *[t for q in range(4) for t in g_free[q]])
        return back

    crsr_free = ffn2(0, ("attn", 8))

    t_m = load(mask[:, 0:384], A["band"], VE.now)
    VE.wait(t_m)
    QK, KK, VV, OO, PT3 = X0, X0 + 2, X0 + 4, 0, X0 + 6
    k3 = {}
    fr3 = (PE.now,)
    VE.wait(*crsr_free)
    evac_first = [lambda _, ps, t, j=j: rope_tile(KK + j, ps, t, cr, sr, fr3,
                                                          lambda y: k3.update({KK + j: y})) for j in range(2)]
    evac_first += [evac_v(VV + j, ("v", j, VV + j)) for j in range(2)]

    def proj_q(j):
        yield from linear("s_q", 1, 8, rhs_u, 1, lambda _, ps, t: rope_tile(QK + j % 2, ps, t, cr, sr, (PE.now,),
                                                                            lambda y: qk_tok.update({("q3", j): y})),
                          LB2, first=j, hooks={3: flush_turns})

    def gen3():
        for j in range(1, 8):
            yield from proj_q(j)

    run(linear("s_first", 4, 8, rhs_u, 4, lambda j, ps, t: evac_first[j](0, ps, t), [0, 1, 2, 3], hooks={6: cols_now, 7: begin}))
    flush_turns()
    run(proj_q(0))
    ahead = gen3()
    for _ in range(5):
        next(ahead)
    flush()

    def drain3():
        t_uf = PE.now
        ev_o[0] = resid(("ffn", 8), lambda: (t_uf,))
        yield from as_ready(linear("s_o4", 4, 8, lambda k: (*hl(OO + k), o_tok[k]), 4, ev_o[0], [0, 1, 2, 3]),
                            lambda k: len(o_tok.get(k, ())) == 4)

    o_tok.clear()

    def moff(i):
        return 128 if i == 0 else 0

    def head_of(t):
        j, r = t // 2, t % 2
        return j, r

    def kv_of(t):
        return (t // 2) // 4

    def O3(t, ps, tok, sched):
        j, r = t // 2, 64 * (t % 2)
        oh, ol = (z[r:r + 64, :] for z in hl(OO + j))
        src = ps[r:r + 64, :]
        hi = AC.do(lambda e: e.activation(oh, src, ACT.Copy), tok)

        def low():
            lo = VE.do(lambda e: e.tensor_tensor(ol, src, oh.bitcast(F), ALU.subtract), hi)
            bank_free[obk] = (lo,)
            o_tok[j] = o_tok.get(j, ()) + (hi, lo)
        sched(1, low)

    attention("swa", 16, 4, 3, 2,
              lambda t: (*hl(QK + (t // 2) % 2), 64 * (t % 2), qk_tok[("q3", t // 2)]),
              lambda t: (*hl(KK + kv_of(t)), 64 * (t % 2), k3[KK + kv_of(t)]),
              lambda t: (*hl(VV + kv_of(t)), qk_tok[("v", kv_of(t), VV + kv_of(t))]),
              lambda i: (max(0, 128 * i - 128), min(S, 128 * i + 256)), O3, ahead, lambda s: 1, PT3, drain3)
    flush()
    stat["rb_free"] = (VE.now,)
    run(linear("s_o1", 1, 8, lambda k: (*hl(OO + k), o_tok[k]), 4, lambda j, ps, t: ev_o[0](4 + j, ps, t), LB7))
    flush()
    ffn2(1, None)

    cols_now()
    spread_now()
    s_out = sem("out")
    for k in range(NC):
        v = VE.do(lambda e, k=k: e.scalar_tensor_tensor(out=h[:, k, :], in0=h[:, k, :], scalar=vc("final", k),
                                                        in1=rb[:, :], op0=ALU.mult, op1=ALU.mult),
                  stat["rb"], *h_tok[k])
        if k % 2:
            SP.wait(v)
            SP.q.append(lambda e, k=k: e.dma_start(out[:, k - 1:k + 1, :], h[:, k - 1:k + 1, :]).then_inc(s_out, 16))
    SP.wait((s_out, 16 * 4))

    if dry:
        return
    assert st["used"] == total, (st["used"], total)
    block = ctx.enter_context(nc.Block())
    block.sync(SP.run)
    block.gpsimd(GP.run)
    block.scalar(AC.run)
    block.tensor(PE.run)
    block.vector(VE.run)


def lay(w, G):
    K, N = w.shape
    kk = 4 // G
    u = w.reshape(K // 128 // kk, kk, 128, N // (128 * G), 128 * G).transpose(3, 0, 2, 1, 4).reshape(-1, 2, 128, 512)
    return np.ascontiguousarray(u.transpose(0, 2, 1, 3)).reshape(-1, 128, 1024)


def lay_blocks(w, n, G):
    return np.concatenate([lay(w[i:i + n], G) for i in range(0, w.shape[0], n)])


def half_interleave(w):
    K, N = w.shape
    return w.reshape(K, N // 64, 2, 2, 16).transpose(0, 1, 3, 2, 4).reshape(K, N)


SWA_ORDER = [4 * (2 * (j // 4) + r) + j % 4 for j in range(8) for r in range(2)]


def columns(v):
    v = v.reshape(-1, v.shape[-1])
    return np.concatenate([r.reshape(-1, 128).T for r in v], axis=1)


def shape_constants():
    inv = (np.float32(10000.0) ** (-np.arange(0, 64, 2, dtype=np.float32) / np.float32(64))).astype(np.float32)
    p = np.arange(128)
    invf = inv[(p % 64) // 32 * 16 + p % 16][:, None]
    sgn = np.where(p % 32 < 16, -1.0, 1.0).astype(np.float32)[:, None]
    hd = 2 * np.arange(4)[None, :] + (p // 64)[:, None]
    qs = (2.0 ** (hd + 1 - 3)).astype(np.float32)
    t = np.arange(16)
    icnt = np.concatenate([1.0 / np.minimum(t + 1, w) for w in (2, 4, 8, 16)]).astype(np.float32)
    icnt = np.broadcast_to(icnt, (128, 64))
    c = np.arange(512)[None, :] - 384
    d = (p[:, None] - c).astype(np.float32)
    alibi = np.where(d >= 0, -d, np.float32(-BIG)).astype(np.float32)
    c = np.arange(384)[None, :] - 128
    band = np.where(np.abs(c - p[:, None]) <= 128, 0.0, -BIG).astype(np.float32)
    return invf, sgn, qs, icnt, alibi, band


def layout(i):
    i = {k: np.asarray(v) for k, v in i.items()}
    invf, sgn, qs, icnt, alibi, band = shape_constants()
    a = {}
    a["x"] = np.ascontiguousarray(i["x"][0].T.reshape(8, 128, 512).transpose(1, 0, 2))
    a["pos"] = np.ascontiguousarray(np.broadcast_to(i["positions_2"], (128, 512)))
    a["p"] = np.ascontiguousarray(i["p_2"][:, 0].transpose(0, 2, 1).reshape(2, 2, 128, 512).transpose(0, 2, 1, 3))
    a["alibi"], a["band"] = alibi, band
    so = np.array(SWA_ORDER)
    a["vec"] = np.ascontiguousarray(np.concatenate(
        [columns(i[n]) for n in ("norm_mix_pre", "b_gate", "pool_scale", "norm_mix_post", "norm_mlp_pre",
                                 "norm_mlp_post", "attn_norm_2", "ffn_norm_2", "ple_norm_2", "final_norm_2",
                                 "diff_subln_2", "ffn_conv_w_2", "ffn_conv_b_2")]
        + [np.broadcast_to(i["swa_sinks_2"][0][so], (128, 16)), invf, sgn, qs, icnt], axis=1))
    a["lam"] = np.ascontiguousarray(np.broadcast_to(i["diff_lambda_2"][0].reshape(256), (128, 256)))
    w = i["w_in"][0]
    a["w_p"], a["w_q"], a["w_k"], a["w_v"] = (lay(w[:, 512 * n:512 * n + 512], 1) for n in range(4))
    a["w_first"] = lay(np.concatenate([w[:, n:n + 128] for n in (512, 1024, 1536, 0)], axis=1), 4)
    for n in ("w_p", "w_q", "w_k", "w_v"):
        a[n] = np.ascontiguousarray(a[n][1:])
    a["w_gp"], a["w_ga"] = lay(w[:, 2048:3072], 2), lay(w[:, 3072:4096], 2)
    a["pool_w"] = np.ascontiguousarray(i["pool_w"][0].transpose(1, 0, 2)).reshape(128, 512)
    a["w_bp"], a["w_ba"] = lay(i["w_branch_pool"][0], 2), lay(i["w_branch_attn"][0], 2)
    a["w_out4"], a["w_out1"] = lay(i["w_out"][0][:, :512], 4), lay(i["w_out"][0][:, 512:], 1)
    a["w_up"] = lay(i["w_up"][0], 4)
    a["w_down"] = lay_blocks(i["w_down"][0], 512, 1)
    w = i["diff_w_qkv_2"][0]
    a["d_q"], a["d_k"], a["d_v"] = (lay(half_interleave(w[:, :1024]), 1), lay(half_interleave(w[:, 1024:2048]), 1),
                                    lay(w[:, 2048:], 1))
    wq, wk = half_interleave(w[:, :256]), half_interleave(w[:, 1024:1152])
    a["d_first"] = lay(np.concatenate([wq[:, :128], wk, w[:, 2048:2176], wq[:, 128:]], axis=1), 4)
    for n, t in (("d_q", 2), ("d_k", 1), ("d_v", 1)):
        a[n] = np.ascontiguousarray(a[n][t:])
    w = i["diff_w_o_2"][0]
    a["d_o4"], a["d_o1"] = lay(w[:, :512], 4), lay(w[:, 512:], 1)
    w = i["swa_w_qkv_2"][0]
    wq = w[:, :1024].reshape(1024, 16, 64)[:, so].reshape(1024, 1024)
    a["s_q"] = lay(half_interleave(wq), 1)
    a["s_first"] = lay(np.concatenate([half_interleave(w[:, 1024:1280]), w[:, 1280:]], axis=1), 4)
    w = i["swa_w_o_2"][0].reshape(16, 64, 1024)[so].reshape(1024, 1024)
    a["s_o4"], a["s_o1"] = lay(w[:, :512], 4), lay(w[:, 512:], 1)
    for l in range(2):
        w = i["ffn_w_up_2"][l]
        a[f"f_g{l}"], a[f"f_g{l}t"] = lay(w[:, :2560], 4), lay(w[:, 2560:2816], 2)
        a[f"f_v{l}"], a[f"f_v{l}t"] = lay(w[:, 2816:5376], 4), lay(w[:, 5376:], 2)
        w = i["ffn_w_down_2"][l]
        a[f"f_d{l}"], a[f"f_d{l}t"] = lay_blocks(w[:2560], 512, 1), lay(w[2560:], 2)
        a[f"p_p{l}"] = lay(i["ple_w_proj_2"][l], 4)
        w = i["ple_w_gate_2"][l]
        a[f"p_g{l}4"], a[f"p_g{l}1"] = lay(w[:, :512], 4), lay(w[:, 512:], 1)
    return a


def kernel(**inputs):
    import concourse.bacc as bacc
    from concourse.bass_utils import run_bass_kernel_spmd

    nc = bacc.Bacc("TRN2", target_bir_lowering=False, num_devices=1)
    arrays = {f"in_{k}": v for k, v in layout(inputs).items()}
    aps = {k[3:]: nc.dram_tensor(k, v.shape, mybir.dt.from_np(v.dtype), kind="ExternalInput").ap()
           for k, v in arrays.items()}
    out = nc.dram_tensor("out_dram", (128, 8, 512), F, kind="ExternalOutput").ap()
    program(nc, aps, out)
    r = run_bass_kernel_spmd(nc, [arrays], core_ids=[0])
    got = r.results[0]["out_dram"]
    return np.ascontiguousarray(got.transpose(1, 0, 2).reshape(1024, 512).T)[None]
```

```python
from contextlib import ExitStack

import numpy as np
import concourse.bass as bass
from concourse import mybir

F = mybir.dt.float32
R = mybir.dt.float32r
I32 = mybir.dt.int32
ACT = mybir.ActivationFunctionType
ALU = mybir.AluOpType
AX = mybir.AxisListType.X

S = 512
NC = 8
EPS = 1e-6
BIG = 3.0e38
NU = 6
LOOK = 4
NP = 3
NT = 5
FF2 = 22

V_COLS = {}


def vec_layout():
    at = 0
    for name, n in (("mix_pre", 8), ("b_gate", 16), ("pool_scale", 4), ("mix_post", 8), ("mlp_pre", 8),
                    ("mlp_post", 8), ("attn", 16), ("ffn", 16), ("ple", 16), ("final", 8), ("subln", 1),
                    ("cw", 264), ("cb", 88), ("sinks", 16), ("invf", 1), ("sgn", 1), ("qs", 4),
                    ("icnt", 64)):
        V_COLS[name] = at
        at += n
    return at


NV = vec_layout()


class Eng:

    def __init__(self, key, sem):
        self.key, self.sem, self.n, self.q, self.seen = key, sem, 0, [], {}

    def wait(self, *tokens):
        for t in tokens:
            if t is None:
                continue
            sem, v = t
            if self.seen.get(sem.name, 0) < v:
                self.seen[sem.name] = v
                self.q.append(lambda e, s=sem, v=v: e.wait_ge(s, v))

    def do(self, f, *tokens, sig=True):
        self.wait(*tokens)
        if not sig:
            self.q.append(f)
            return None
        self.n += 1
        self.q.append(lambda e, f=f: f(e).then_inc(self.sem, 1))
        return (self.sem, self.n)

    @property
    def now(self):
        return (self.sem, self.n) if self.n else None

    def run(self, e):
        for f in self.q:
            f(e)


class Pool:

    def __init__(self, views):
        self.views, self.free = dict(enumerate(views)), [(i, ()) for i in range(len(views))]

    def get(self):
        assert self.free, "no buffer is free"
        i, tokens = self.free.pop(0)
        return i, self.views[i], tokens

    def release(self, i, *tokens):
        self.free.append((i, tokens))

    def lend(self, views, *tokens):
        for v in views:
            i = len(self.views)
            self.views[i] = v
            self.free.append((i, tokens))

    def take_back(self, first):
        gone = [x for x in self.free if x[0] >= first]
        self.free = [x for x in self.free if x[0] < first]
        assert len(gone) == len(self.views) - first
        for i, _ in gone:
            del self.views[i]
        return [t for _, ts in gone for t in ts]


def program(nc, A, out):
    order = []
    with ExitStack() as c0:
        build(nc, A, out, None, order, c0, dry=True)
    with ExitStack() as c1:
        build(nc, A, out, order, [], c1, dry=False)


def build(nc, A, out, plan, seen_units, ctx, dry):
    tag = "d" if dry else "m"

    def sb(name, shape, dt):
        return ctx.enter_context(nc.sbuf_tensor(tag + name, shape, dt))

    def sem(name):
        return ctx.enter_context(nc.semaphore(tag + name))

    PE, VE, AC, GP, SP = (Eng(k, sem("s_" + k)) for k in ("pe", "ve", "ac", "gp", "sp"))

    ra = sb("ra", [128, 32, 2, S], R)
    h = sb("h", [128, NC, S], F)
    raw = sb("raw", [128, NP, 2, S], F)
    fa = sb("fa", [128, 8, S], F)
    tmp = sb("tmp", [128, NT, S], F)
    ssq = sb("ssq", [128, S], F)
    rb = sb("rb", [128, S], F)
    mask = sb("mask", [128, S], F)
    rope = sb("rope", [128, 2, S], F)
    ident = sb("ident", [128, 128], F)
    ones = sb("ones", [128, 128], F)
    vec = sb("vec", [128, NV], F)
    sm = sb("sm", [128, 96], F)
    smi = sb("smi", [128, 4], I32)
    gbuf = sb("gbuf", [128, 4, S], F)
    cr = sb("cr", [128, S], F)[:, :]
    sr = sb("sr", [128, S], F)[:, :]
    banks = [ctx.enter_context(nc.psum_tensor(f"{tag}b{i}", [128, S], F)) for i in range(8)]

    def hl(i):
        return ra[:, i, 0, :], ra[:, i, 1, :]

    def vc(name, i):
        return vec[:, V_COLS[name] + i:V_COLS[name] + i + 1]

    U_A = [hl(i) for i in range(8)]
    U_B = [hl(24 + i) for i in range(8)]
    U = list(U_A)
    WS = [hl(8 + i) for i in range(NU)]
    X0 = 8 + NU

    bank_free = [()] * 8

    dsem = [sem(f"d{i}") for i in range(NP)]
    st = dict(dma=0, split=0, used=0)
    raw_free = [()] * NP
    unit_tok = {}
    unit_free = {}
    total = len(plan) * 2 if plan else 0

    def emit_dma(n):
        slot = n % NP
        SP.wait(*raw_free[slot])
        name, i = plan[n]
        SP.q.append(lambda e: e.dma_start(raw[:, slot, :, :].rearrange("p a b -> p (a b)"),
                                          A[name][i]).then_inc(dsem[slot], 16))

    def emit_split(u):
        n = u // 2
        slot = n % NP
        landed = (dsem[slot], 16 * (n // NP + 1))
        src = raw[:, slot, u % 2, :]
        wh, wl = WS[u % NU]
        freed = unit_free.get(u - NU)
        th = AC.do(lambda e: e.activation(wh, src, ACT.Copy), landed, freed)
        tl = GP.do(lambda e: e.tensor_tensor(wl, src, wh.bitcast(F), ALU.subtract), landed, freed, th)
        unit_tok[u] = (th, tl)
        if u % 2:
            raw_free[slot] = (tl,)
            if n + NP < len(plan):
                emit_dma(n + NP)

    def next_unit(name, idx):
        u = st["used"]
        st["used"] += 1
        if u % 2 == 0:
            seen_units.append((name, idx // 2))
        if plan is None:
            return u, WS[u % NU], (None, None)
        assert plan[u // 2] == (name, idx // 2), (plan[u // 2], name, idx)
        while st["split"] < min(total, u + 1 + min(LOOK, 1 + u)):
            emit_split(st["split"])
            st["split"] += 1
        return u, WS[u % NU], unit_tok[u]

    bg = []
    bgn = [0]

    def later(f):
        bg.append(f)

    def tick(n):
        bgn[0] += n
        if bgn[0] >= 9:
            bgn[0] = 0
            if bg:
                bg.pop(0)()

    def flush():
        while bg:
            bg.pop(0)()

    def linear(name, G, K, rhs, ntiles, evac, lb, first=0, hooks=None, order=None):
        kk = 4 // G
        base = first * K // 4
        done = []
        step = 0
        for g in range(ntiles // G):
            bs = []
            for _ in range(G):
                b = lb.pop(0)
                lb.append(b)
                bs.append(b)
            for b in bs:
                PE.wait(*bank_free[b])
                bank_free[b] = None
            for ku in range(K // kk):
                u, (wh, wl), tok = next_unit(name, order[ku] if order else base + g * (K // kk) + ku)
                for q in range(kk):
                    k = ku * kk + q
                    xh, xl, xt = rhs(k)
                    PE.wait(*tok, *xt)
                    for j in range(G):
                        c = (q * G + j) * 128
                        ps = banks[bs[j]][:, :]
                        a, l = wh[:, c:c + 128], wl[:, c:c + 128]
                        PE.do(lambda e, ps=ps, a=a, x=xh, s=(k == 0): e.matmul(ps, a, x, start=s, stop=False), sig=False)
                        PE.do(lambda e, ps=ps, a=a, x=xl: e.matmul(ps, a, x, start=False, stop=False), sig=False)
                        last = PE.do(lambda e, ps=ps, l=l, x=xh, s=(k == K - 1): e.matmul(ps, l, x, start=False, stop=s))
                        if k == K - 1:
                            done.append((j, ps, last))
                    if q == kk - 1:
                        unit_free[u] = last
                    if hooks and step in hooks:
                        hooks[step]()
                    for j, ps, t in done:
                        bank_free[bs[j]] = evac(first + g * G + j, ps, t)
                    done.clear()
                    step += 1
                    tick(3 * G)
                    yield

    def run(gen):
        for _ in gen:
            pass

    clock = [0]

    def outputs(name, part, ready, evac, opens):
        def one(n):
            return linear(name, 2, 8, part, 2, lambda j, ps, t: evac(j, ps, t), [2 * n, 2 * n + 1], first=2 * n,
                          order=[3 * n, 3 * n + 1, 3 * n + 2, 9 + n])
        gens = [one(n) for n in range(len(opens))]
        for n, g in enumerate(gens):
            while clock[0] < opens[n] or None in (bank_free[2 * n], bank_free[2 * n + 1]):
                yield
            for k in range(6):
                while not ready(k | 1):
                    yield
                next(g)
                yield
                yield
        while not ready(7):
            yield
        for g in gens:
            for _ in g:
                yield

    T = Pool([tmp[:, i, :] for i in range(NT)])
    T.lend([gbuf[:, i, :] for i in range(4)])

    def split(dst, src, tok, eng=None, free=()):
        dh, dl = dst
        a = AC.do(lambda e: e.activation(dh, src, ACT.Copy), *tok, *free)
        b = (eng or VE).do(lambda e: e.tensor_tensor(dl, src, dh.bitcast(F), ALU.subtract), *tok, a, *free)
        return a, b

    STB = 7

    def rstd_cols(src, tok, D, col):
        PE.wait(*bank_free[STB], *tok)
        ps = banks[STB]
        for i in range(4):
            t = PE.do(lambda e, i=i: e.matmul(ps[:, i:i + 1], src[:, 128 * i:128 * i + 128], ones[:, 0:1],
                                              start=True, stop=True))
        bank_free[STB] = None
        x, y, a = sm[:, col + 4:col + 8], sm[:, col:col + 4], sm[:, col + 8:col + 12]
        v = VE.do(lambda e: e.tensor_scalar(x, ps[:, 0:4], 1.0 / D, EPS, ALU.mult, ALU.add), t, VE.now)
        bank_free[STB] = (v,)
        v = VE.do(lambda e: e.tensor_scalar(smi[:, :], x.bitcast(I32), 1, None, ALU.arith_shift_right), v)
        v = VE.do(lambda e: e.tensor_scalar(y.bitcast(I32), smi[:, :], -1.0, float(0x5F3759DF), ALU.mult, ALU.add), v)
        for _ in range(3):
            v = VE.do(lambda e: e.tensor_tensor(a, y, y, ALU.mult), v)
            v = VE.do(lambda e: e.scalar_tensor_tensor(out=a, in0=a, scalar=-0.5, in1=x, op0=ALU.mult, op1=ALU.mult), v)
            v = VE.do(lambda e: e.scalar_tensor_tensor(out=y, in0=a, scalar=1.5, in1=y, op0=ALU.add, op1=ALU.mult), v)
        return v

    def spread(col, tok):
        PE.wait(tok, *bank_free[STB])
        for q in range(4):
            t = PE.do(lambda e, q=q: e.matmul(banks[STB][:, 128 * q:128 * q + 128],
                                              sm[:, col + q:col + q + 1].to_broadcast([128, 128]), ident[:, :],
                                              start=True, stop=True))
        bank_free[STB] = None
        return t

    stat = dict(n=0, rb_free=(), ssq_free=())

    def add_square(src, tok, eng=None):
        if stat["n"] == 0:
            stat["tok"] = AC.do(lambda e: e.activation(ssq[:, :], src, ACT.Square), *tok, *stat["ssq_free"])
        else:
            i, q, free = T.get()
            a = AC.do(lambda e: e.activation(q, src, ACT.Square), *tok, *free)
            stat["tok"] = (eng or VE).do(lambda e: e.tensor_tensor(ssq[:, :], ssq[:, :], q, ALU.add), a, stat["tok"])
            T.release(i, stat["tok"])
        stat["n"] += 1

    def cols_now():
        assert stat["n"] == NC
        stat["cols"] = rstd_cols(ssq, (stat["tok"],), 1024.0, 0)
        stat["ssq_free"] = (PE.now,)
        stat["n"] = 0

    def spread_now():
        t = spread(0, stat["cols"])
        stat["rb"] = AC.do(lambda e: e.activation(rb[:, :], banks[STB][:, :], ACT.Copy), t, *stat["rb_free"])
        bank_free[STB] = (stat["rb"],)

    nin = [0]

    def load(dst, src, *tok):
        SP.wait(*tok)
        s = sem(f"in{nin[0]}")
        nin[0] += 1
        SP.q.append(lambda e: e.dma_start(dst, src).then_inc(s, 16))
        return (s, 16)

    h_tok = [(load(h[:, 0, :], A["x"][:, 0, :]),)]
    t_vec = load(vec[:, :], A["vec"])
    for n, (a, b) in enumerate(((1, 2), (2, 4), (4, 6), (6, 8))):
        if plan and n < NP:
            emit_dma(n)
        h_tok += [(load(h[:, a:b, :], A["x"][:, a:b, :]),)] * (b - a)
    t_cst = load(mask[:, :], A["alibi"])
    t1 = GP.do(lambda e: e.memset(ident[:, :], 0.0))
    t_ones = GP.do(lambda e: e.memset(ones[:, :], 1.0))
    t_id = GP.do(lambda e: e.affine_select(out=ident[:, :], in_=ident[:, :], compare_op=ALU.not_equal, fill=1.0,
                                           base=0, pattern=[[-1, 128]], channel_multiplier=1), t1)
    PE.wait(t_id, t_ones)
    VE.wait(t_id)
    AC.wait(t_vec)
    VE.wait(t_vec)

    u_tok = [None] * NC

    def make_u(k, gain, free, eng=None):
        uh, ul = U[k]
        g = vc(*gain)
        a = AC.do(lambda e: e.activation(uh, h[:, k, :], ACT.Copy, scale=g), *h_tok[k], *free)

        def rest():
            b = VE.do(lambda e: e.scalar_tensor_tensor(out=ul, in0=h[:, k, :], scalar=g, in1=uh.bitcast(F),
                                                       op0=ALU.mult, op1=ALU.subtract), a, *h_tok[k], *free)
            u_tok[k] = (a, b)
            add_square(h[:, k, :], h_tok[k], eng)
        return rest

    pending = []
    made = [0]

    def rhs_u(k):
        if k == 0:
            made[0] = 0
        while pending and made[0] <= k + 2:
            pending.pop(0)()
            made[0] += 1
        return (*U[k], u_tok[k])

    def queue_inputs(produce):
        rest = [None]

        def chain(k):
            nr = produce(k) if k < NC else None
            if k == 0:
                nr = nr()
            if rest[0]:
                rest[0]()
            rest[0] = nr
        for k in range(NC + 1):
            pending.append(lambda k=k: chain(k))

    queue_inputs(lambda k: make_u(k, ("mix_pre", k), ()))

    two_pi = 2 * np.pi

    def piece(x, bits=12):
        m, ex = np.frexp(x)
        return float(np.ldexp(np.round(m * 2.0 ** bits), int(ex) - bits))

    c1 = piece(two_pi)
    c2 = piece(two_pi - c1)
    c3 = float(np.float32(two_pi - c1 - c2))
    magic = 1.5 * 2.0 ** 23
    t_rope = []

    def rope_table(which, shift, add):
        def f():
            (i0, ang, f0), (i1, n1, f1), (i2, nh, f2), (i3, r, f3) = (T.get() for _ in range(4))
            t_pos = load(ang.bitcast(I32), A["pos"], *f0)
            VE.wait(*f1, *f2, *f3)
            v = VE.do(lambda e: e.tensor_copy(r, ang.bitcast(I32)), t_pos)
            v = VE.do(lambda e: e.tensor_scalar(ang, r, vc("invf", 0), None, ALU.mult), v)
            v = VE.do(lambda e: e.tensor_scalar(n1, ang, float(1 / two_pi), shift, ALU.mult, ALU.add), v)
            v = VE.do(lambda e: e.tensor_scalar(n1, n1, magic, None, ALU.add), v)
            v = VE.do(lambda e: e.tensor_scalar(n1, n1, magic, None, ALU.subtract), v)
            v = VE.do(lambda e: e.tensor_scalar(nh, n1, 2.0 ** -12, magic, ALU.mult, ALU.add), v)
            v = VE.do(lambda e: e.tensor_scalar(nh, nh, magic, None, ALU.subtract), v)
            v = VE.do(lambda e: e.scalar_tensor_tensor(out=n1, in0=nh, scalar=-4096.0, in1=n1,
                                                       op0=ALU.mult, op1=ALU.add), v)
            src = ang
            for cc in (c1, c2, c3):
                v = VE.do(lambda e, cc=cc, src=src: e.scalar_tensor_tensor(
                    out=r, in0=nh, scalar=-4096.0 * cc, in1=src, op0=ALU.mult, op1=ALU.add), v)
                v = VE.do(lambda e, cc=cc: e.scalar_tensor_tensor(
                    out=r, in0=n1, scalar=-cc, in1=r, op0=ALU.mult, op1=ALU.add), v)
                src = r
            v = VE.do(lambda e: e.tensor_scalar(r, r, add, None, ALU.add), v)
            v = VE.do(lambda e: e.tensor_scalar(r, r, 3.1415925, -3.1415925, ALU.min, ALU.max), v)
            dst = rope[:, which, :]

            def sine(v=v):
                v = AC.do(lambda e: e.activation(dst, r, ACT.Sin), v)
                if which:
                    v = VE.do(lambda e: e.tensor_scalar(dst, dst, vc("sgn", 0), None, ALU.mult), v)
                for i in (i0, i1, i2, i3):
                    T.release(i, v)
                t_rope.append(v)
            for _ in range(5):
                later(lambda: None)
            later(sine)
        return f

    sbk = [2, 3]
    tbk = [4, 5]
    obk = 6

    def rot(l):
        b = l.pop(0)
        l.append(b)
        return b

    SWAP = [(i + 16) % 32 for i in range(32)]

    def attention(kind, nun, spu, lat_t, lat_v, Q, KT, VT, span, O, gen, rate, PTb):
        acts = {}
        order = [0]
        PRI = (0.6, 3, 0.55, 0.7, 3.5)

        def at(slot, f, pri=1):
            order[0] += 1
            acts.setdefault(slot, []).append((pri, order[0], f))

        P = [[fa[:, 4 * b + i, :] for i in range(4)] for b in range(2)]
        p_free = {}
        pt = [[ra[:, PTb + 2 * p + z, :, :].rearrange("p a (b c) -> p (a b) c", b=2)
               for z in range(2)] for p in range(2)]
        pt_free = [(), ()]
        p_tok = {}
        small = {}

        def s_tile(t, i, comp=None):
            lo, hi = span(i)
            n = hi - lo
            b = rot(sbk)
            ps = banks[b][:, 0:n]
            qh, ql, row, qt = Q(t)
            kh, kl, krow, kt_ = KT(t)
            if comp is not None:
                row = krow = 64 * comp
            assert row == krow
            PE.wait(*bank_free[b], *qt, *kt_)
            bank_free[b] = None
            qs, ks = slice(128 * i, 128 * i + 128), slice(lo, hi)
            rr = slice(row, row + 64)
            PE.do(lambda e: e.matmul(ps, qh[rr, qs], kh[rr, ks], start=True, stop=False), sig=False)
            PE.do(lambda e: e.matmul(ps, ql[rr, qs], kh[rr, ks], start=False, stop=False), sig=False)
            return b, ps, n, PE.do(lambda e: e.matmul(ps, qh[rr, qs], kl[rr, ks], start=False, stop=True))

        def soft(t, i):
            k = (t % 2) * 4 + i
            free2 = p_free.get((k, "s"), ())
            d = {}
            if kind == "diff":
                base = 24 + 8 * (k % 4)
                a = P[t % 2][i]
                ti, pb, tfree = T.get()
                mx, nm, su = (sm[:, base + 2 * z:base + 2 * z + 2] for z in range(3))
                parts = []
                for comp in range(2):
                    b, ps, n, ts = s_tile(t, i, comp)
                    v = VE.do(lambda e, mx=mx[:, comp:comp + 1], ps=ps: e.reduce_max(mx, ps, AX), ts, *free2)
                    parts.append((b, (a, pb)[comp], ps, comp, (p_free.get(k, ()), tfree)[comp]))

                def bias():
                    d["m"] = VE.do(lambda e: e.tensor_scalar(nm, mx, -0.125, None, ALU.mult), v)

                def expo():
                    for b, dst, ps, c, fr in parts:
                        d["x"] = AC.do(lambda e, dst=dst, ps=ps, c=slice(c, c + 1): e.activation(
                            dst, ps, ACT.Exp, bias=nm[:, c], scale=0.125, accum_out=su[:, c]), d["m"], *fr)
                        bank_free[b] = (d["x"],)

                def norm1():
                    d["r"] = VE.do(lambda e: e.reciprocal(su, su), d["x"])

                def norm2():
                    d["l"] = VE.do(lambda e: e.tensor_scalar(su[:, 1:2], su[:, 1:2], lam, None, ALU.mult), d["r"])

                def norm3():
                    v = VE.do(lambda e: e.tensor_scalar(a, a, su[:, 0:1], None, ALU.mult), d["r"])
                    v = VE.do(lambda e: e.scalar_tensor_tensor(out=a, in0=pb, scalar=su[:, 1:2], in1=a, op0=ALU.mult,
                                                               op1=ALU.add), v, d["l"])
                    T.release(ti, v)
                    p_free[(k, "s")] = (v,)
                    p_tok[(t, i)] = v
                return bias, expo, norm1, norm2, norm3
            base = 24 + 4 * k
            mx, nm, su, es = (sm[:, base + z:base + z + 1] for z in range(4))
            lo, hi = span(i)
            a = P[t % 2][i][:, 0:hi - lo]
            b, ps, n, ts = s_tile(t, i)
            off = moff(i)
            m = mask[:, off:off + n]
            v = VE.do(lambda e: e.tensor_tensor_reduce(a, ps, m, 1.0, -BIG, ALU.add, ALU.max, mx), ts,
                      *p_free.get(k, ()), *free2)
            bank_free[b] = (v,)
            if kind == "moba":
                sl, s8 = 2.0 ** -(t + 1), -BIG
            else:
                sl, s8 = 0.125, sink8[:, t:t + 1]

            def bias():
                d["m"] = VE.do(lambda e: e.tensor_scalar(nm, mx, s8, -sl, ALU.max, ALU.mult), v)

            def expo():
                d["x"] = AC.do(lambda e: e.activation(a, a, ACT.Exp, bias=nm, scale=sl, accum_out=su), d["m"])
                if kind != "moba":
                    d["x"] = AC.do(lambda e: e.activation(es, vc("sinks", t), ACT.Exp, bias=nm), d["m"])

            def norm1():
                if kind != "moba":
                    d["x"] = VE.do(lambda e: e.tensor_tensor(su, su, es, ALU.add), d["x"])

            def norm2():
                d["r"] = VE.do(lambda e: e.reciprocal(su, su), d["x"])

            def norm3():
                v = VE.do(lambda e: e.tensor_scalar(a, a, su, 1.0, ALU.mult, ALU.mult), d["r"])
                p_free[(k, "s")] = (v,)
                p_tok[(t, i)] = v
            return bias, expo, norm1, norm2, norm3

        def turn(t, i):
            k = (t % 2) * 4 + i
            lo, hi = span(i)
            n = (hi - lo) // 128
            b = rot(tbk)
            PE.wait(*bank_free[b], p_tok[(t, i)])
            a = P[t % 2][i]
            ps = banks[b]
            for q in range(n):
                x = PE.do(lambda e, q=q: e.transpose(ps[:, 128 * q:128 * q + 128], a[:, 128 * q:128 * q + 128],
                                                     ident[:, :]))
            p_free[k] = (x,)
            k0 = lo // 128
            h0 = 128 * (i % 2)
            dst = [pt[i // 2][z][:, k0:k0 + n, h0:h0 + 128] for z in range(2)]
            src = ps[:, 0:128 * n].rearrange("p (a b) -> p a b", b=128)
            free = pt_free[i // 2] if i % 2 == 0 else ()
            hi = AC.do(lambda e: e.activation(dst[0], src, ACT.Copy), x, *free)
            bank_free[b] = None

            def low():
                lo = VE.do(lambda e: e.tensor_tensor(dst[1], src, dst[0].bitcast(F), ALU.subtract), hi)
                bank_free[b] = (lo,)
                small[(t, i)] = (hi, lo)
            sched(1, low)

        def pv(t, pr):
            vh, vl, vt = VT(t)
            PE.wait(*vt, *small[(t, 2 * pr)], *small[(t, 2 * pr + 1)])
            if pr == 0:
                PE.wait(*bank_free[obk])
                bank_free[obk] = None
            ps = banks[obk]
            parts = []
            for kt in range(4):
                qs = [i for i in (2 * pr, 2 * pr + 1) if span(i)[0] <= 128 * kt < span(i)[1]]
                if qs:
                    parts.append((-len(qs), kt, 128 * (qs[0] % 2), 128 * (qs[-1] % 2) + 128))
            parts.sort()
            first = True
            for w, (_, kt, a, b) in enumerate(parts):
                vs = slice(128 * kt, 128 * kt + 128)
                ph, pl = (pt[pr][z][:, kt, a:b] for z in range(2))
                dst = ps[:, 256 * pr + a:256 * pr + b]
                for z, (vv, pp) in enumerate(((vh, ph), (vh, pl), (vl, ph))):
                    last = PE.do(lambda e, vv=vv, pp=pp, dst=dst, vs=vs, s=first, f=(z == 2 and w == len(parts) - 1):
                                 e.matmul(dst, vv[:, vs], pp, start=s, stop=f, skip_group_check=True))
                    first = False
            pt_free[pr] = (last,)
            if pr == 1:
                O(t, ps, last, sched)

        now = [0]

        def sched(d, f):
            at(now[0] + d, f, 0)

        def start(slot, t, i):
            bias, expo, norm1, norm2, norm3 = soft(t, i)
            at(slot, bias, PRI[1])
            at(slot + 1, expo, 1)
            for p, f in zip(PRI[2:], (norm1, norm2, norm3)):
                at(slot + 2, f, p)

        for t in range(nun):
            step = spu // 4
            t0 = spu * t + lat_t
            for i in range(4):
                at(spu * t + step * i, lambda t=t, i=i, s=spu * t + step * i: start(s, t, i), PRI[0])
                at(t0 + step * i, lambda t=t, i=i: turn(t, i), 1)
            at(t0 + step + lat_v, lambda t=t: pv(t, 0), 0)
            at(t0 + 3 * step + lat_v, lambda t=t: pv(t, 1), 0)
        live = True
        slot = 0
        while slot <= max(acts):
            now[0] = clock[0] = slot
            for _ in range(rate(slot)):
                if live and next(gen, "end") == "end":
                    live = False
            if not live:
                tick(9)
            todo = acts.get(slot, [])
            while todo:
                todo.sort(key=lambda z: z[:2])
                todo.pop(0)[2]()
            slot += 1
        run(gen)
        return PE.now, VE.now, AC.now

    def v_tile(dst, ps, tok):
        i, z, free = T.get()
        v = VE.do(lambda e: e.tensor_tensor(z, ps, rb[:, :], ALU.mult), tok, stat["rb"], *free)

        def turn_v():
            b = rot(tbk)
            PE.wait(*bank_free[b], v)
            for q in range(4):
                x = PE.do(lambda e, q=q: e.transpose(banks[b][:, 128 * q:128 * q + 128], z[:, 128 * q:128 * q + 128],
                                                     ident[:, :]))
            T.release(i, x)
            vtoks[dst] = split(hl(dst), banks[b][:, :], (x,), free=())
            bank_free[b] = vtoks[dst]
        return v, turn_v

    vtoks = {}

    def rope_tile(dst, ps, tok, cr, sr, free, done, eng=None):
        i, sh, f1 = T.get()
        j, t1_, f2 = T.get()
        a = VE.do(lambda e: e.stream_shuffle(sh, ps, SWAP), tok, *f1)
        b = VE.do(lambda e: e.tensor_tensor(t1_, ps, cr, ALU.mult), tok, *f2, t_cr[0])
        first = eng is not None
        eng = eng or GP
        g = eng.do(lambda e: e.tensor_tensor(sh, sh, sr, ALU.mult), a, t_cr[0])
        g = eng.do(lambda e: e.tensor_tensor(t1_, t1_, sh, ALU.add), b, g)
        T.release(i, g)
        def parts():
            y = split(hl(dst), t1_, (g,), eng=VE if first else GP, free=free)
            T.release(j, *y)
            done(y)
        later(lambda: None)
        later(parts)
        return (b, a)

    t_cr = [None]

    QK = X0
    VV = X0 + 4
    OO = X0 + 6
    PY = X0 + 10
    PT1 = X0 + 14
    qk_tok = {}

    def moff(i):
        return 384 - 128 * i

    def evac_q1(j):
        def f(_, ps, tok):
            i, z, free = T.get()
            v = VE.do(lambda e: e.scalar_tensor_tensor(out=z, in0=ps, scalar=vc("qs", j), in1=rb[:, :],
                                                       op0=ALU.mult, op1=ALU.mult), tok, stat["rb"], *free)

            def parts():
                y = split(hl(QK + (j % 2) * 2), z, (v,), eng=GP, free=(PE.now,))
                T.release(i, *y)
                qk_tok[("q", j)] = y
            later(parts)
            return (v,)
        return f

    def evac_k1(j):
        def f(_, ps, tok):
            i, z, free = T.get()
            v = VE.do(lambda e: e.tensor_tensor(z, ps, rb[:, :], ALU.mult), tok, stat["rb"], *free)

            def parts():
                y = split(hl(QK + (j % 2) * 2 + 1), z, (v,), eng=GP, free=(PE.now,))
                T.release(i, *y)
                qk_tok[("k", j)] = y
            later(parts)
            return (v,)
        return f

    def evac_v(dst, key):
        def f(_, ps, tok):
            v, turn_v = v_tile(dst, ps, tok)
            turns.append((turn_v, key))
            return (v,)
        return f

    turns = []
    LB2 = [0, 1]

    p_in = {}

    def evac_p(g, ps, tok):
        i0, x, f0 = T.get()
        v = VE.do(lambda e: e.tensor_tensor(x, ps, rb[:, :], ALU.mult), tok, stat["rb"], *f0)
        freed = v
        d = {}

        def double(r):
            if r == 0:
                (i1, a, f1), (i2, b, f2) = T.get(), T.get()
                VE.wait(*f1, *f2)
                d.update(src=x, dst=a, oth=b, ids=(i0, i1, i2), v=v)
            src, dst, w = d["src"], d["dst"], 1 << r
            VE.do(lambda e: e.tensor_tensor(dst[:, w:S], src[:, w:S], src[:, 0:S - w], ALU.add), d["v"])
            d["v"] = VE.do(lambda e: e.tensor_copy(dst[:, 0:w], src[:, 0:w]), d["v"])
            d["src"], d["dst"], d["oth"] = dst, d["oth"], dst

        def mean():
            src, dst = d["src"], d["dst"]
            w = 2 << g
            c = V_COLS["icnt"] + 16 * g
            u = VE.do(lambda e: e.tensor_tensor(dst[:, 0:16], src[:, 0:16], vec[:, c:c + 16], ALU.mult), d["v"])
            u = VE.do(lambda e: e.tensor_tensor(dst[:, 0:16], dst[:, 0:16], x[:, 0:16], ALU.subtract), u)
            u = VE.do(lambda e: e.scalar_tensor_tensor(out=dst[:, 16:S], in0=src[:, 16:S], scalar=1.0 / w,
                                                       in1=x[:, 16:S], op0=ALU.mult, op1=ALU.subtract), u)
            d["v"] = u

        def parts():
            p_in[g] = split(hl(PY + g), d["dst"], (d["v"],), eng=GP)
            for i in d["ids"]:
                T.release(i, *p_in[g])
        for r in range(g + 1):
            later(lambda r=r: double(r))
        later(mean)
        later(parts)
        return (freed,)

    def flush_turns():
        while turns:
            f, key = turns.pop(0)
            f()
            qk_tok[key] = vtoks[key[2]]

    def proj1(j, hooks=None):
        lb = LB2
        n = 0
        for name, ev in (("w_q", evac_q1(j)), ("w_k", evac_k1(j)), ("w_v", evac_v(VV + j % 2, ("v", j, VV + j % 2)))):
            for _ in linear(name, 1, 8, rhs_u, 1, ev, lb, first=j - 1, hooks=hooks if n == 0 else None):
                n += 1
                if n % 8 == 3:
                    flush_turns()
                yield

    LB7 = [0, 1, 2, 3, 4, 5, 6]
    evac_first = (evac_v(VV, ("v", 0, VV)), evac_q1(0), evac_k1(0), lambda _, ps, t: evac_p(0, ps, t))
    run(linear("w_first", 4, 8, rhs_u, 4, lambda j, ps, t: evac_first[j](0, ps, t), [0, 1, 2, 3],
               hooks={6: cols_now, 7: spread_now}))

    def gen1():
        for j in range(1, 4):
            yield from proj1(j)
        yield from linear("w_p", 1, 8, rhs_u, 3, lambda j, ps, t: evac_p(j + 1, ps, t), LB2, hooks={2: flush_turns})
        flush_turns()

    o_tok = {}

    def O1(t, ps, tok, sched):
        j, r = t // 2, 64 * (t % 2)
        oh, ol = (z[r:r + 64, :] for z in hl(OO + j))
        src = ps[r:r + 64, :]
        hi = AC.do(lambda e: e.activation(oh, src, ACT.Copy), tok)

        def low():
            lo = VE.do(lambda e: e.tensor_tensor(ol, src, oh.bitcast(F), ALU.subtract), hi)
            bank_free[obk] = (lo,)
            o_tok[j] = o_tok.get(j, ()) + (hi, lo)
        sched(1, low)

    def Q1(t):
        j = t // 2
        return (*hl(QK + (j % 2) * 2), 64 * (t % 2), qk_tok[("q", j)])

    def K1(t):
        j = t // 2
        return (*hl(QK + (j % 2) * 2 + 1), 64 * (t % 2), qk_tok[("k", j)])

    def V1(t):
        j = t // 2
        return (*hl(VV + j % 2), qk_tok[("v", j, VV + j % 2)])

    ahead = gen1()
    for _ in range(6):
        next(ahead)
    flush()
    pw_i, pw_raw, pw_free = T.get()
    VE.wait(t_cst)
    t_pw = load(pw_raw, A["pool_w"], *pw_free)
    att_done = attention("moba", 8, 4, 3, 2, Q1, K1, V1, lambda i: (0, 128 * (i + 1)), O1, ahead, lambda s: (2 if s < 6 else 3) if s < 24 else 2, PT1)

    pwh, pwl = hl(PT1 + 2)
    pw_tok = split((pwh, pwl), pw_raw, (t_pw,), free=(att_done[0],))
    T.release(pw_i, *pw_tok)

    def pool_products():
        for g in range(4):
            b = rot(LB7)
            gh, gl = hl(PY + g)
            PE.wait(*bank_free[b], *pw_tok, *p_in[g])
            ps = banks[b]
            cs = slice(128 * g, 128 * g + 128)
            PE.do(lambda e, ps=ps, cs=cs, gh=gh: e.matmul(ps[:, :], pwh[:, cs], gh, start=True, stop=False), sig=False)
            PE.do(lambda e, ps=ps, cs=cs, gl=gl: e.matmul(ps[:, :], pwh[:, cs], gl, start=False, stop=False), sig=False)
            t = PE.do(lambda e, ps=ps, cs=cs, gh=gh: e.matmul(ps[:, :], pwl[:, cs], gh, start=False, stop=True))
            i, z, free = T.get()
            v = VE.do(lambda e, ps=ps, z=z, g=g: e.tensor_scalar(z, ps[:, :], vc("pool_scale", g), None, ALU.mult), t, *free)
            bank_free[b] = (v,)
            p_in[g] = split(hl(PY + g), z, (v,), free=(t,))
            T.release(i, *p_in[g])

    MM = [QK + i for i in range(6)] + [PT1, PT1 + 1]
    m_tok = {}
    t_mm = PE.now
    sg = {}

    def evac_g(base):
        def f(j, ps, tok):
            i, z, free = T.get()
            v = VE.do(lambda e: e.tensor_tensor(z, ps, rb[:, :], ALU.mult), tok, stat["rb"], *free)
            a = AC.do(lambda e: e.activation(z, z, ACT.Sigmoid, bias=vc("b_gate", base + j)), v)
            sg[(base, j)] = (i, z, a)
            return (v,)
        return f

    def evac_bp(j, ps, tok):
        i, z, a = sg[(0, j)]
        v = VE.do(lambda e: e.tensor_tensor(z, ps, z, ALU.mult), tok, a)
        sg[(0, j)] = (i, z, v)
        return (v,)

    def evac_ba(j, ps, tok):
        i, z, a = sg[(8, j)]
        i0, z0, a0 = sg[(0, j)]
        v = VE.do(lambda e: e.tensor_tensor(z, ps, z, ALU.mult), tok, a)
        w = VE.do(lambda e: e.tensor_tensor(z, z, z0, ALU.add), v, a0)
        T.release(i0, w)
        m_tok[j] = split(hl(MM[j]), z, (w,), free=(t_mm,))
        T.release(i, *m_tok[j])
        return (v,)

    rhs_p = lambda k: (*hl(PY + k), p_in[k])
    rhs_o1 = lambda k: (*hl(OO + k), o_tok[k])
    for jj in range(4):
        if jj == 0:
            flush()
        run(linear("w_gp", 2, 8, rhs_u, 2, evac_g(0), LB7, first=2 * jj))
        run(linear("w_ga", 2, 8, rhs_u, 2, evac_g(8), LB7, first=2 * jj))
        if jj == 0:
            pool_products()
        run(linear("w_bp", 2, 4, rhs_p, 2, evac_bp, LB7, first=2 * jj))
        run(linear("w_ba", 2, 4, rhs_o1, 2, evac_ba, LB7, first=2 * jj))
    stat["rb_free"] = (VE.now,)
    t_u_free = PE.now

    def y_chunk(j):
        return fa[:, j, :]

    y_tok = {}

    def evac_y(j, ps, tok):
        a = AC.do(lambda e: e.activation(y_chunk(j), ps, ACT.Copy), tok)
        y_tok[j] = a
        add_square(y_chunk(j), (a,))
        return (a,)

    def post_norm(gain, nxt, u_free):
        cols_now()
        spread_now()
        def produce(k):
            i, z, free = T.get()
            v = VE.do(lambda e: e.tensor_tensor(z, y_chunk(k), rb[:, :], ALU.mult), stat["rb"], y_tok[k], *free)
            v = VE.do(lambda e: e.scalar_tensor_tensor(out=h[:, k, :], in0=z, scalar=vc(gain, k),
                                                       in1=h[:, k, :], op0=ALU.mult, op1=ALU.add), v)
            T.release(i, v)
            h_tok[k] = (v,)
            if k == NC - 1:
                stat["rb_free"] = (VE.now,)
            return make_u(k, (nxt[0], nxt[1] + k), u_free, GP)

        queue_inputs(produce)

    rhs_m = lambda k: (*hl(MM[k]), m_tok[k])
    AC.wait(*att_done)
    run(linear("w_out4", 4, 8, rhs_m, 4, evac_y, LB7))
    run(linear("w_out1", 1, 8, rhs_m, 4, lambda j, ps, t: evac_y(4 + j, ps, t), LB7))
    post_norm("mix_post", ("mlp_pre", 0), (t_u_free,))

    def a_slot(blk, q):
        return X0 + (blk % 2) * 4 + q

    a_tok = {}
    a_free = {}

    def start_hooks(late=False):
        return {6: cols_now, 7: spread_now} if late else {3: cols_now, 5: spread_now}

    def evac_up(blk):
        def f(j, ps, tok):
            q = j - 4 * blk
            i, z, free = T.get()
            v = VE.do(lambda e: e.scalar_tensor_tensor(out=z, in0=ps, scalar=0.0, in1=rb[:, :], op0=ALU.max,
                                                       op1=ALU.mult), tok, stat["rb"], *free)
            a = AC.do(lambda e: e.activation(z, z, ACT.Square), v)
            a_tok[(blk, q)] = split(hl(a_slot(blk, q)), z, (a,), free=a_free.get(blk - 2, ()))
            T.release(i, *a_tok[(blk, q)])
            return (v,)
        return f

    def evac_acc(first, last, done):
        def f(j, ps, tok):
            dst = y_chunk(j)
            if first:
                y_tok[j] = AC.do(lambda e: e.activation(dst, ps, ACT.Copy), tok, *h_tok[j])
                t = y_tok[j]
            else:
                t = y_tok[j] = VE.do(lambda e: e.tensor_tensor(dst, ps, dst, ALU.add), tok, y_tok[j])
            if last:
                done(j)
            return (t,)
        return f

    lam = sm[:, 92:93]
    sink8 = sm[:, 76:92]
    subg = sm[:, 93:94]

    def small_consts():
        i, z, free = T.get()
        t = load(z[:, 0:256], A["lam"], *free)
        L = z[:, 0:256].rearrange("p (a b c) -> p a b c", a=2, b=2)
        v = VE.do(lambda e: e.tensor_tensor(z[:, 256:384].rearrange("p (a c) -> p a c", a=2), L[:, :, 0, :], L[:, :, 1, :],
                                            ALU.mult), t)
        v = VE.do(lambda e: e.reduce_sum(z[:, 384:386], z[:, 256:384].rearrange("p (a b) -> p a b", b=64), AX), v)
        a = AC.do(lambda e: e.activation(z[:, 386:388], z[:, 384:386], ACT.Exp), v)
        v = VE.do(lambda e: e.tensor_tensor(lam, z[:, 387:388], z[:, 386:387], ALU.subtract), a)
        v = VE.do(lambda e: e.tensor_scalar(lam, lam, -0.2, None, ALU.add), v)
        T.release(i, v)
        s = V_COLS["sinks"]
        v = VE.do(lambda e: e.tensor_scalar(sink8, vec[:, s:s + 16], 8.0, None, ALU.mult), v)
        VE.do(lambda e: e.tensor_scalar(subg, vc("subln", 0), 0.8, None, ALU.mult))

    t_a0 = PE.now
    a_free[-2] = a_free[-1] = (t_a0,)
    NB = 8
    for b in range(NB + 1):
        if b < NB:
            run(linear("w_up", 4, 8, rhs_u, 4, evac_up(b), LB7, first=4 * b, hooks={0: start_hooks(True), 2: {1: rope_table(0, 0.25, float(np.pi / 2))}, 4: {1: rope_table(1, 0.0, 0.0)}, 6: {1: small_consts}}.get(b)))
        if b >= 1:
            rh = lambda k, b=b: (*hl(a_slot(b - 1, k)), a_tok[(b - 1, k)])
            run(linear("w_down", 1, 4, rh, 8, lambda j, ps, t, b=b: evac_acc(
                b == 1, b == NB, lambda q: add_square(y_chunk(q), (y_tok[q],)))(j - 8 * (b - 1), ps, t),
                LB7, first=8 * (b - 1)))
            a_free[b - 1] = (PE.now,)
    stat["rb_free"] = (VE.now,)
    post_norm("mlp_post", ("attn", 0), (PE.now,))

    def fold_rope():
        a = VE.do(lambda e: e.tensor_tensor(cr, rope[:, 0, :], rb[:, :], ALU.mult), stat["rb"], *t_rope)
        b = VE.do(lambda e: e.tensor_tensor(sr, rope[:, 1, :], rb[:, :], ALU.mult), stat["rb"])
        t_cr[0] = b

    QK, VV, OO, PT2 = X0, X0 + 4, X0 + 6, X0 + 14
    o_tok2 = {}

    def begin():
        spread_now()
        fold_rope()


    def resid(nxt, free):
        def f(j, ps, tok):
            v = VE.do(lambda e: e.tensor_tensor(h[:, j, :], ps, h[:, j, :], ALU.add), tok, *h_tok[j])
            h_tok[j] = (v,)
            later(lambda: later_u(j, nxt, free()))
            return (v,)
        return f

    def later_u(j, nxt, free):
        bg.insert(min(1, len(bg)), make_u(j, (nxt[0], nxt[1] + j), free))

    ev_o = [None]

    def proj2(hd):
        base = QK + (hd % 2) * 2
        n = 0
        for name, ev in ((
            ("d_q", lambda _, ps, t: rope_tile(base, ps, t, cr, sr, (PE.now,),
                                           lambda y: qk_tok.update({("q2", hd): y}))),
            ("d_k", lambda _, ps, t: rope_tile(base + 1, ps, t, cr, sr, (PE.now,),
                                           lambda y: qk_tok.update({("k2", hd): y}))),
            ("d_v", evac_v(VV + hd % 2, ("v", hd, VV + hd % 2))),
        )[1 if hd == 1 else 0:]):
            for _ in linear(name, 1, 8, rhs_u, 1, ev, LB2, first=hd - (2 if name == "d_q" else 1)):
                n += 1
                if n % 8 == 3:
                    flush_turns()
                yield

    rt2 = lambda j, dst, d, eng=None: lambda _, ps, t: rope_tile(dst, ps, t, cr, sr, (), lambda y: qk_tok.update({d: y}), eng)
    evac_first = (evac_v(VV, ("v", 0, VV)), rt2(0, QK, ("q2", 0), GP), rt2(0, QK + 1, ("k2", 0), VE),
                  rt2(1, QK + 2, ("q2", 1)))
    run(linear("d_first", 4, 8, rhs_u, 4, lambda j, ps, t: evac_first[j](0, ps, t), [0, 1, 2, 3],
               hooks={6: cols_now, 7: begin}))

    def gen2():
        for j in range(1, 8):
            yield from proj2(j)
        flush_turns()
        t_uf = PE.now
        ev_o[0] = resid(("ffn", 0), lambda: (t_uf,))
        yield from outputs("d_o", lambda k: (*hl(OO + k), o_tok2[k]), lambda k: k in o_tok2, ev_o[0], (0, 64, 68))

    ahead = gen2()
    for _ in range(8):
        next(ahead)
    flush()

    def O2(t, ps, tok, sched):
        i, z, f1 = T.get()
        z_t = VE.do(lambda e: e.tensor_copy(z, ps[:, :]), tok, *f1)
        bank_free[obk] = (z_t,)
        d = {}

        def square():
            d["j"], d["q"], f2 = T.get()
            d["a"] = AC.do(lambda e: e.activation(d["q"], z, ACT.Square), z_t, *f2)

        def stats():
            d["v"] = rstd_cols(d["q"], (d["a"],), 128.0, 12)
            T.release(d["j"], PE.now)

        def scale():
            s = spread(12, d["v"])
            d["w"] = VE.do(lambda e: e.scalar_tensor_tensor(out=z, in0=z, scalar=subg, in1=banks[STB][:, :],
                                                            op0=ALU.mult, op1=ALU.mult), s, z_t)
            bank_free[STB] = (d["w"],)

        def parts():
            o_tok2[t] = split(hl(OO + t), z, (d["w"],))
            T.release(i, *o_tok2[t])
        for n, f in ((1, square), (2, stats), (4, scale), (5, parts)):
            sched(n, f)

    attention("diff", 8, 8, 4, 3,
              lambda t: (*hl(QK + (t % 2) * 2), 0, qk_tok[("q2", t)]),
              lambda t: (*hl(QK + (t % 2) * 2 + 1), 0, qk_tok[("k2", t)]),
              lambda t: (*hl(VV + t % 2), qk_tok[("v", t, VV + t % 2)]),
              lambda i: (0, S), O2, ahead, lambda s: 1 if s < 8 else 3 if s < 64 else 2, PT2)
    flush()

    stat["rb_free"] = (VE.now,)
    run(linear("d_o", 2, 8, lambda k: (*hl(OO + k), o_tok2[k]), 2, ev_o[0], LB7, first=6))
    flush()

    def ffn2(l, nxt_gain):
        gv = {}
        VAL = X0

        def evac_conv(b, val, n):
            def f(j, ps, tok):
                ch = j + (FF2 if val else 0)
                w = [vc("cw", (l * 3 + z) * 2 * FF2 + ch) for z in range(3)]
                cb = vc("cb", l * 2 * FF2 + ch)
                i, z, f1 = T.get()
                q = (j - 4 * b)
                v = VE.do(lambda e: e.tensor_tensor(z, ps, rb[:, :], ALU.mult), tok, stat["rb"], *f1)
                d = {}

                def one():
                    if val:
                        d["i"], d["y"], f2 = T.get()
                    else:
                        d["y"], f2 = g_buf[q], g_free.get(q, ())
                    y = d["y"]
                    d["a"] = AC.do(lambda e: e.activation(y, z, ACT.Identity, scale=w[1], bias=cb), v, *f2)

                def two():
                    y = d["y"]
                    x = VE.do(lambda e: e.scalar_tensor_tensor(out=y[:, 1:S], in0=z[:, 0:S - 1], scalar=w[0],
                                                               in1=y[:, 1:S], op0=ALU.mult, op1=ALU.add), d["a"])
                    x = VE.do(lambda e: e.scalar_tensor_tensor(out=y[:, 0:S - 1], in0=z[:, 1:S], scalar=w[2],
                                                               in1=y[:, 0:S - 1], op0=ALU.mult, op1=ALU.add), x)
                    if val:
                        T.release(i, x)
                        gb = g_buf[q]
                        x = VE.do(lambda e: e.tensor_tensor(y, y, gb, ALU.mult), x, gv[(b, q)])
                        g_free[q] = (x,)
                    d["x"] = x

                def three():
                    y = d["y"]
                    if val:
                        a_tok[(b, q)] = split(hl(a_slot(b, q)), y, (d["x"],), free=a_free.get(b - 2, ()))
                        T.release(d["i"], *a_tok[(b, q)])
                    else:
                        s = AC.do(lambda e: e.activation(z, y, ACT.Sigmoid), d["x"])
                        gt = GP.do(lambda e: e.tensor_tensor(y, y, z, ALU.mult), s)
                        T.release(i, gt)
                        gv[(b, q)] = gt

                tiles.append((one, two, three))
                if len(tiles) == n:
                    ts = list(tiles)
                    tiles.clear()
                    for s in range(n + 2):
                        later(lambda s=s: [ts[s - z][z]() for z in (2, 1, 0) if 0 <= s - z < n])
                return (v,)
            return f

        tiles = []
        g_buf = [gbuf[:, q, :] for q in range(4)]
        back = tuple(T.take_back(NT))
        T.lend([cr, sr], VE.now, GP.now)
        g_free = {q: back for q in range(4)}
        pts = []
        for k in range(2):
            i, z, free = T.get()
            t_p = load(z, A["p"][l][:, k, :], *free)
            pts.append(split(hl(X0 + 8 + k), z, (t_p,), free=(PE.now,)))
            T.release(i, *pts[k])
        a_free.clear()
        a_free[-2] = a_free[-1] = (PE.now,)
        y_tok.clear()
        NBK = 6
        for b in range(NBK + 1):
            if b < NBK:
                G = 4 if b < 5 else 2
                sfx = "" if G == 4 else "t"
                fst = 4 * b if G == 4 else 0
                off = 0 if G == 4 else 20
                run(linear(f"f_g{l}{sfx}", G, 8, rhs_u, G, lambda j, ps, t: evac_conv(b, False, G)(j + off, ps, t), LB7,
                           first=fst, hooks=start_hooks() if b == 0 else None))
                run(linear(f"f_v{l}{sfx}", G, 8, rhs_u, G, lambda j, ps, t: evac_conv(b, True, G)(j + off, ps, t), LB7,
                           first=fst))
            if b >= 1:
                K = 4 if b - 1 < 5 else 2
                rh = lambda k, b=b: (*hl(a_slot(b - 1, k)), a_tok[(b - 1, k)])
                last = b == NBK
                u_free = (PE.now,)

                def done(q):
                    v = VE.do(lambda e, q=q: e.tensor_tensor(h[:, q, :], y_chunk(q), h[:, q, :], ALU.add),
                              y_tok[q], *h_tok[q])
                    h_tok[q] = (v,)
                    later(lambda: later_u(q, ("ple", 8 * l), u_free))

                if K == 4:
                    run(linear(f"f_d{l}", 1, 4, rh, 8, lambda j, ps, t, b=b: evac_acc(b == 1, last, done)(
                        j - 8 * (b - 1), ps, t), LB7, first=8 * (b - 1)))
                else:
                    run(linear(f"f_d{l}t", 2, 2, rh, 8, lambda j, ps, t: evac_acc(False, last, done)(j, ps, t), LB7))
                a_free[b - 1] = (PE.now,)
        stat["rb_free"] = (VE.now,)
        flush()
        pl = {}

        def evac_pp(j, ps, tok):
            pl[j] = AC.do(lambda e: e.activation(y_chunk(j), ps, ACT.Copy), tok, *h_tok[j])
            return (pl[j],)

        rp = lambda k: (*hl(X0 + 8 + k), pts[k])
        ub_free = (PE.now,)
        def evac_pg(j, ps, tok):
            i, z, f1 = T.get()
            v = VE.do(lambda e: e.tensor_tensor(z, ps, rb[:, :], ALU.mult), tok, stat["rb"], *f1)
            a = AC.do(lambda e: e.activation(z, z, ACT.Sigmoid), v)
            m = VE.do(lambda e: e.tensor_tensor(z, z, y_chunk(j), ALU.mult), a, pl[j])
            m = VE.do(lambda e: e.tensor_tensor(h[:, j, :], h[:, j, :], z, ALU.add), m, *h_tok[j])
            T.release(i, m)
            h_tok[j] = (m,)
            if nxt_gain is None:
                later(lambda: add_square(h[:, j, :], h_tok[j]))
            else:
                later(lambda: later_u(j, nxt_gain, ub_free))
            return (v,)

        run(linear(f"p_p{l}", 4, 2, rp, 8, evac_pp, LB7, hooks={3: cols_now}))
        Uc, uc = list(U), list(u_tok)
        rhs_g = lambda k: (*Uc[k], uc[k])
        if nxt_gain:
            U[:] = U_B
        run(linear(f"p_g{l}4", 4, 8, rhs_g, 4, evac_pg, LB7, hooks={1: spread_now}))
        run(linear(f"p_g{l}1", 1, 8, rhs_g, 4, lambda j, ps, t: evac_pg(4 + j, ps, t), LB7))
        flush()
        stat["rb_free"] = (VE.now,)
        back = tuple(T.take_back(NT))
        T.lend([gbuf[:, q, :] for q in range(4)], *[t for q in range(4) for t in g_free[q]])
        return back

    crsr_free = ffn2(0, ("attn", 8))

    t_m = load(mask[:, 0:384], A["band"], VE.now)
    VE.wait(t_m)
    QK, KK, VV, OO, PT3 = X0, X0 + 2, X0 + 4, 0, X0 + 6
    k3 = {}
    fr3 = (PE.now,)
    VE.wait(*crsr_free)
    evac_first = [evac_v(VV + j, ("v", j, VV + j)) for j in range(2)]
    evac_first += [lambda _, ps, t, j=j: rope_tile(KK + j, ps, t, cr, sr, fr3, lambda y: k3.update({KK + j: y}),
                                                      (GP, VE)[j])
                   for j in range(2)]

    def proj_q(j):
        yield from linear("s_q", 1, 8, rhs_u, 1, lambda _, ps, t: rope_tile(QK + j % 2, ps, t, cr, sr, (PE.now,),
                                                                            lambda y: qk_tok.update({("q3", j): y})),
                          LB2, first=j, hooks={3: flush_turns})

    def gen3():
        for j in range(1, 8):
            yield from proj_q(j)
        t_uf = PE.now
        ev_o[0] = resid(("ffn", 8), lambda: (t_uf,))
        yield from outputs("s_o", lambda k: (*hl(OO + k), o_tok[k]), lambda k: len(o_tok.get(k, ())) == 4, ev_o[0],
                           (0, 64, 68))

    run(linear("s_first", 4, 8, rhs_u, 4, lambda j, ps, t: evac_first[j](0, ps, t), [0, 1, 2, 3],
               hooks={6: cols_now, 7: begin}))
    run(proj_q(0))
    ahead = gen3()
    for _ in range(7):
        next(ahead)
    flush()

    o_tok.clear()

    def moff(i):
        return 128 if i == 0 else 0

    def kv_of(t):
        return (t // 2) // 4

    def O3(t, ps, tok, sched):
        j, r = t // 2, 64 * (t % 2)
        oh, ol = (z[r:r + 64, :] for z in hl(OO + j))
        src = ps[r:r + 64, :]
        hi = AC.do(lambda e: e.activation(oh, src, ACT.Copy), tok)

        def low():
            lo = VE.do(lambda e: e.tensor_tensor(ol, src, oh.bitcast(F), ALU.subtract), hi)
            bank_free[obk] = (lo,)
            o_tok[j] = o_tok.get(j, ()) + (hi, lo)
        sched(1, low)

    attention("swa", 16, 4, 3, 2,
              lambda t: (*hl(QK + (t // 2) % 2), 64 * (t % 2), qk_tok[("q3", t // 2)]),
              lambda t: (*hl(KK + kv_of(t)), 64 * (t % 2), k3[KK + kv_of(t)]),
              lambda t: (*hl(VV + kv_of(t)), qk_tok[("v", kv_of(t), VV + kv_of(t))]),
              lambda i: (max(0, 128 * i - 128), min(S, 128 * i + 256)), O3, ahead, lambda s: 1 if s < 64 else 2, PT3)
    flush()
    stat["rb_free"] = (VE.now,)
    run(linear("s_o", 2, 8, lambda k: (*hl(OO + k), o_tok[k]), 2, ev_o[0], LB7, first=6))
    flush()
    ffn2(1, None)

    cols_now()
    t = spread(0, stat["cols"])
    s_out = sem("out")
    for k in range(NC):
        v = VE.do(lambda e, k=k: e.scalar_tensor_tensor(out=h[:, k, :], in0=h[:, k, :], scalar=vc("final", k),
                                                        in1=banks[STB][:, :], op0=ALU.mult, op1=ALU.mult), t, *h_tok[k])
        if k % 2:
            SP.wait(v)
            SP.q.append(lambda e, k=k: e.dma_start(out[:, k - 1:k + 1, :], h[:, k - 1:k + 1, :]).then_inc(s_out, 16))
    SP.wait((s_out, 16 * 4))

    if dry:
        return
    assert st["used"] == total, (st["used"], total)
    block = ctx.enter_context(nc.Block())
    block.sync(SP.run)
    block.gpsimd(GP.run)
    block.scalar(AC.run)
    block.tensor(PE.run)
    block.vector(VE.run)


def lay(w, G):
    K, N = w.shape
    kk = 4 // G
    u = w.reshape(K // 128 // kk, kk, 128, N // (128 * G), 128 * G).transpose(3, 0, 2, 1, 4).reshape(-1, 2, 128, 512)
    return np.ascontiguousarray(u.transpose(0, 2, 1, 3)).reshape(-1, 128, 1024)


def lay_blocks(w, n, G):
    return np.concatenate([lay(w[i:i + n], G) for i in range(0, w.shape[0], n)])


def lay_outputs(w):
    u = lay(w, 2).reshape(8, 128, 2, 512).transpose(0, 2, 1, 3).reshape(16, 128, 512)
    u = u[[0, 1, 2, 4, 5, 6, 8, 9, 10, 3, 7, 11, 12, 13, 14, 15]].reshape(8, 2, 128, 512)
    return np.ascontiguousarray(u.transpose(0, 2, 1, 3)).reshape(8, 128, 1024)


def half_interleave(w):
    K, N = w.shape
    return w.reshape(K, N // 64, 2, 2, 16).transpose(0, 1, 3, 2, 4).reshape(K, N)


SWA_ORDER = [4 * (2 * (j // 4) + r) + j % 4 for j in range(8) for r in range(2)]


def columns(v):
    v = v.reshape(-1, v.shape[-1])
    return np.concatenate([r.reshape(-1, 128).T for r in v], axis=1)


def shape_constants():
    inv = (np.float32(10000.0) ** (-np.arange(0, 64, 2, dtype=np.float32) / np.float32(64))).astype(np.float32)
    p = np.arange(128)
    invf = inv[(p % 64) // 32 * 16 + p % 16][:, None]
    sgn = np.where(p % 32 < 16, -1.0, 1.0).astype(np.float32)[:, None]
    hd = 2 * np.arange(4)[None, :] + (p // 64)[:, None]
    qs = (2.0 ** (hd + 1 - 3)).astype(np.float32)
    t = np.arange(16)
    icnt = np.concatenate([1.0 / np.minimum(t + 1, w) for w in (2, 4, 8, 16)]).astype(np.float32)
    icnt = np.broadcast_to(icnt, (128, 64))
    c = np.arange(512)[None, :] - 384
    d = (p[:, None] - c).astype(np.float32)
    alibi = np.where(d >= 0, -d, np.float32(-BIG)).astype(np.float32)
    c = np.arange(384)[None, :] - 128
    band = np.where(np.abs(c - p[:, None]) <= 128, 0.0, -BIG).astype(np.float32)
    return invf, sgn, qs, icnt, alibi, band


def layout(i):
    i = {k: np.asarray(v) for k, v in i.items()}
    invf, sgn, qs, icnt, alibi, band = shape_constants()
    a = {}
    a["x"] = np.ascontiguousarray(i["x"][0].T.reshape(8, 128, 512).transpose(1, 0, 2))
    a["pos"] = np.ascontiguousarray(np.broadcast_to(i["positions_2"], (128, 512)))
    a["p"] = np.ascontiguousarray(i["p_2"][:, 0].transpose(0, 2, 1).reshape(2, 2, 128, 512).transpose(0, 2, 1, 3))
    a["alibi"], a["band"] = alibi, band
    so = np.array(SWA_ORDER)
    a["vec"] = np.ascontiguousarray(np.concatenate(
        [columns(i[n]) for n in ("norm_mix_pre", "b_gate", "pool_scale", "norm_mix_post", "norm_mlp_pre",
                                 "norm_mlp_post", "attn_norm_2", "ffn_norm_2", "ple_norm_2", "final_norm_2",
                                 "diff_subln_2", "ffn_conv_w_2", "ffn_conv_b_2")]
        + [np.broadcast_to(i["swa_sinks_2"][0][so], (128, 16)), invf, sgn, qs, icnt], axis=1))
    a["lam"] = np.ascontiguousarray(np.broadcast_to(i["diff_lambda_2"][0].reshape(256), (128, 256)))
    w = i["w_in"][0]
    a["w_p"], a["w_q"], a["w_k"], a["w_v"] = (lay(w[:, 512 * n:512 * n + 512], 1) for n in range(4))
    a["w_first"] = lay(np.concatenate([w[:, n:n + 128] for n in (1536, 512, 1024, 0)], axis=1), 4)
    for n in ("w_p", "w_q", "w_k", "w_v"):
        a[n] = np.ascontiguousarray(a[n][1:])
    a["w_gp"], a["w_ga"] = lay(w[:, 2048:3072], 2), lay(w[:, 3072:4096], 2)
    a["pool_w"] = np.ascontiguousarray(i["pool_w"][0].transpose(1, 0, 2)).reshape(128, 512)
    a["w_bp"], a["w_ba"] = lay(i["w_branch_pool"][0], 2), lay(i["w_branch_attn"][0], 2)
    a["w_out4"], a["w_out1"] = lay(i["w_out"][0][:, :512], 4), lay(i["w_out"][0][:, 512:], 1)
    a["w_up"] = lay(i["w_up"][0], 4)
    a["w_down"] = lay_blocks(i["w_down"][0], 512, 1)
    w = i["diff_w_qkv_2"][0]
    a["d_q"], a["d_k"], a["d_v"] = (lay(half_interleave(w[:, :1024]), 1), lay(half_interleave(w[:, 1024:2048]), 1),
                                    lay(w[:, 2048:], 1))
    wq, wk = half_interleave(w[:, :256]), half_interleave(w[:, 1024:1152])
    a["d_first"] = lay(np.concatenate([w[:, 2048:2176], wq[:, :128], wk, wq[:, 128:]], axis=1), 4)
    for n, t in (("d_q", 2), ("d_k", 1), ("d_v", 1)):
        a[n] = np.ascontiguousarray(a[n][t:])
    w = i["diff_w_o_2"][0]
    a["d_o"] = lay_outputs(w)
    w = i["swa_w_qkv_2"][0]
    wq = w[:, :1024].reshape(1024, 16, 64)[:, so].reshape(1024, 1024)
    a["s_q"] = lay(half_interleave(wq), 1)
    a["s_first"] = lay(np.concatenate([w[:, 1280:], half_interleave(w[:, 1024:1280])], axis=1), 4)
    w = i["swa_w_o_2"][0].reshape(16, 64, 1024)[so].reshape(1024, 1024)
    a["s_o"] = lay_outputs(w)
    for l in range(2):
        w = i["ffn_w_up_2"][l]
        a[f"f_g{l}"], a[f"f_g{l}t"] = lay(w[:, :2560], 4), lay(w[:, 2560:2816], 2)
        a[f"f_v{l}"], a[f"f_v{l}t"] = lay(w[:, 2816:5376], 4), lay(w[:, 5376:], 2)
        w = i["ffn_w_down_2"][l]
        a[f"f_d{l}"], a[f"f_d{l}t"] = lay_blocks(w[:2560], 512, 1), lay(w[2560:], 2)
        a[f"p_p{l}"] = lay(i["ple_w_proj_2"][l], 4)
        w = i["ple_w_gate_2"][l]
        a[f"p_g{l}4"], a[f"p_g{l}1"] = lay(w[:, :512], 4), lay(w[:, 512:], 1)
    return a


def kernel(**inputs):
    import concourse.bacc as bacc
    from concourse.bass_utils import run_bass_kernel_spmd

    nc = bacc.Bacc("TRN2", target_bir_lowering=False, num_devices=1)
    arrays = {f"in_{k}": v for k, v in layout(inputs).items()}
    aps = {k[3:]: nc.dram_tensor(k, v.shape, mybir.dt.from_np(v.dtype), kind="ExternalInput").ap()
           for k, v in arrays.items()}
    out = nc.dram_tensor("out_dram", (128, 8, 512), F, kind="ExternalOutput").ap()
    program(nc, aps, out)
    r = run_bass_kernel_spmd(nc, [arrays], core_ids=[0])
    got = r.results[0]["out_dram"]
    return np.ascontiguousarray(got.transpose(1, 0, 2).reshape(1024, 512).T)[None]
```
